# Optimizing a Trainium2 kernel written in Bass

```python
import jax, jax.numpy as jnp
from jax import lax
import numpy as np
import math

D_MODEL = 1024
BATCH = 1
SEQ = 512
DEPTH = 1

HEAD_DIM = 64
MIX_WIDTH = D_MODEL
FOX_HEADS = (MIX_WIDTH // 2) // HEAD_DIM
SWA_Q_HEADS = (MIX_WIDTH // 2) // HEAD_DIM
SWA_KV_HEADS = 2
SWA_GROUP = SWA_Q_HEADS // SWA_KV_HEADS
WINDOW = 128
Q_BLOCK = 128
ROPE_THETA = 10000.0
RMS_EPS = 1e-6
FOX_W = FOX_HEADS * HEAD_DIM
SWA_W = SWA_Q_HEADS * HEAD_DIM
SWA_KV_W = SWA_KV_HEADS * HEAD_DIM
IN_SIZES = (FOX_W, FOX_W, FOX_W, FOX_HEADS, FOX_W, SWA_W, SWA_KV_W, SWA_KV_W, SWA_W)
IN_WIDTH = FOX_W * 4 + FOX_HEADS + SWA_W * 2 + SWA_KV_W * 2


def rms_norm(x, g):
    xf = x.astype(jnp.float32)
    y = xf * lax.rsqrt(jnp.mean(xf * xf, axis=-1, keepdims=True) + RMS_EPS)
    return (y * g.astype(jnp.float32)).astype(x.dtype)

def rope(x, positions):
    half = HEAD_DIM // 2
    inv_freq = ROPE_THETA ** (-jnp.arange(half, dtype=jnp.float32) / half)
    ang = positions.astype(jnp.float32)[..., None] * inv_freq
    cos = jnp.cos(ang)[:, :, None, :]
    sin = jnp.sin(ang)[:, :, None, :]
    xf = x.astype(jnp.float32)
    x1, x2 = xf[..., :half], xf[..., half:]
    return jnp.concatenate([x1 * cos - x2 * sin, x2 * cos + x1 * sin], axis=-1).astype(x.dtype)

def forgetting_attention(q, k, v, f_logit):
    B, S, H, d = q.shape
    nb = S // Q_BLOCK
    cum = jnp.cumsum(jax.nn.log_sigmoid(f_logit.astype(jnp.float32)), axis=1)
    cum = cum.transpose(0, 2, 1)
    kh = k.transpose(0, 2, 1, 3)
    vh = v.transpose(0, 2, 1, 3)
    q_blocks = q.transpose(0, 2, 1, 3).reshape(B, H, nb, Q_BLOCK, d).transpose(2, 0, 1, 3, 4)
    c_blocks = cum.reshape(B, H, nb, Q_BLOCK).transpose(2, 0, 1, 3)
    key_pos = jnp.arange(S)
    scale = d ** -0.5

    def one_block(args):
        qb, cb, n = args
        s = jnp.einsum('bhqd,bhkd->bhqk', qb, kh, preferred_element_type=jnp.float32) * scale
        s = s + cb[..., None] - cum[:, :, None, :]
        q_pos = n * Q_BLOCK + jnp.arange(Q_BLOCK)
        causal = key_pos[None, :] <= q_pos[:, None]
        s = jnp.where(causal, s, -jnp.inf)
        p = jax.nn.softmax(s, axis=-1)
        return jnp.einsum('bhqk,bhkd->bhqd', p.astype(vh.dtype), vh)

    out = lax.map(one_block, (q_blocks, c_blocks, jnp.arange(nb)))
    return out.transpose(1, 0, 3, 2, 4).reshape(B, S, H * d)

def sliding_window_sink_attention(q, k, v, sinks):
    B, S, _, d = q.shape
    nb = S // Q_BLOCK
    qb = q.reshape(B, nb, Q_BLOCK, SWA_KV_HEADS, SWA_GROUP, d)

    def with_prev(t):
        t = t.reshape(B, nb, Q_BLOCK, SWA_KV_HEADS, d)
        prev = jnp.pad(t[:, :-1], ((0, 0), (1, 0), (0, 0), (0, 0), (0, 0)))
        return jnp.concatenate([prev, t], axis=2)

    kk, vv = with_prev(k), with_prev(v)
    s = jnp.einsum('bnqhgd,bnshd->bnhgqs', qb, kk, preferred_element_type=jnp.float32) * (d ** -0.5)
    i = jnp.arange(Q_BLOCK)[:, None]
    j = jnp.arange(2 * Q_BLOCK)[None, :]
    rel = i + Q_BLOCK - j
    band = (rel >= 0) & (rel < WINDOW)
    valid_blk = (jnp.arange(nb)[:, None, None] > 0) | (j[None] >= Q_BLOCK)
    mask = band[None] & valid_blk
    s = jnp.where(mask[None, :, None, None], s, -jnp.inf)
    sink = jnp.broadcast_to(
        sinks.astype(jnp.float32).reshape(SWA_KV_HEADS, SWA_GROUP)[None, None, :, :, None, None],
        s.shape[:-1] + (1,))
    p = jax.nn.softmax(jnp.concatenate([s, sink], axis=-1), axis=-1)[..., :-1]
    out = jnp.einsum('bnhgqs,bnshd->bnqhgd', p.astype(vv.dtype), vv)
    return out.reshape(B, S, SWA_Q_HEADS * d)

def first_inputs(seed: int = 0) -> dict:
    key = jax.random.key(seed)
    ks = jax.random.split(key, 12)
    x = jax.random.normal(ks[0], (BATCH, SEQ, D_MODEL), jnp.float32)
    c = jax.random.normal(ks[1], (BATCH, D_MODEL), jnp.float32)
    positions = jnp.broadcast_to(jnp.arange(SEQ, dtype=jnp.int32)[None, :], (BATCH, SEQ))
    w_ada = jax.random.normal(ks[2], (DEPTH, D_MODEL, 3 * D_MODEL), jnp.float32) * (0.5 * D_MODEL ** -0.5)
    b_ada = jax.random.normal(ks[3], (DEPTH, 3 * D_MODEL), jnp.float32) * 0.02
    g_pre = 1.0 + 0.1 * jax.random.normal(ks[4], (DEPTH, D_MODEL), jnp.float32)
    w_in = jax.random.normal(ks[5], (DEPTH, D_MODEL, IN_WIDTH), jnp.float32) * D_MODEL ** -0.5
    b_fgate = jax.random.uniform(ks[6], (DEPTH, FOX_HEADS), jnp.float32, 1.0, 4.0)
    sinks = jax.random.normal(ks[7], (DEPTH, SWA_Q_HEADS), jnp.float32)
    w_out = jax.random.normal(ks[8], (DEPTH, MIX_WIDTH, D_MODEL), jnp.float32) * MIX_WIDTH ** -0.5
    g_post = 1.0 + 0.1 * jax.random.normal(ks[9], (DEPTH, D_MODEL), jnp.float32)
    return {"x": x, "c": c, "positions": positions, "w_ada": w_ada, "b_ada": b_ada,
            "g_pre": g_pre, "w_in": w_in, "b_fgate": b_fgate, "sinks": sinks,
            "w_out": w_out, "g_post": g_post}

def first_block(x, c, positions, w_ada, b_ada, g_pre, w_in, b_fgate, sinks, w_out, g_post):
    B, S, _ = x.shape
    split_points = [int(v) for v in np.cumsum(IN_SIZES)[:-1]]
    for l in range(DEPTH):
        mod = jax.nn.silu(c) @ w_ada[l] + b_ada[l]
        shift, scale, gate = jnp.split(mod, 3, axis=-1)
        h = rms_norm(x, g_pre[l]) * (1.0 + scale[:, None, :]) + shift[:, None, :]
        proj = h @ w_in[l]
        qa, ka, va, fa, za, qb, kb, vb, zb = jnp.split(proj, split_points, axis=-1)
        oa = forgetting_attention(
            qa.reshape(B, S, FOX_HEADS, HEAD_DIM),
            ka.reshape(B, S, FOX_HEADS, HEAD_DIM),
            va.reshape(B, S, FOX_HEADS, HEAD_DIM),
            fa + b_fgate[l])
        oa = oa * jax.nn.silu(za)
        qb = rope(qb.reshape(B, S, SWA_Q_HEADS, HEAD_DIM), positions)
        kb = rope(kb.reshape(B, S, SWA_KV_HEADS, HEAD_DIM), positions)
        ob = sliding_window_sink_attention(qb, kb, vb.reshape(B, S, SWA_KV_HEADS, HEAD_DIM), sinks[l])
        ob = ob * jax.nn.silu(zb)
        y = jnp.concatenate([oa, ob], axis=-1) @ w_out[l]
        x = x + gate[:, None, :] * rms_norm(y, g_post[l])
    return x


MEM_LEN = 256
CONV_CH = D_MODEL
CONV_K = 31
DIFF_HEADS = D_MODEL // 128
DIFF_HEAD_DIM = 64
DIFF_V_DIM = 2 * DIFF_HEAD_DIM
DIFF_WIDTH = DIFF_HEADS * DIFF_V_DIM
X_HEADS = 4
X_HEAD_DIM = D_MODEL // X_HEADS
X_WIDTH = X_HEADS * X_HEAD_DIM
N_BRANCH = 3

IN_SIZES_2 = (
    2 * CONV_CH,
    CONV_CH,
    DIFF_WIDTH,
    DIFF_WIDTH,
    DIFF_WIDTH,
    DIFF_WIDTH,
    X_WIDTH,
    X_WIDTH,
    N_BRANCH * D_MODEL,
)
IN_COLS = sum(IN_SIZES_2)
IN_SPLITS = tuple(int(c) for c in np.cumsum(IN_SIZES_2)[:-1])


def rms_norm_2(x, g, eps=1e-6):
    xf = x.astype(jnp.float32)
    y = xf * lax.rsqrt(jnp.mean(xf * xf, axis=-1, keepdims=True) + eps)
    return (y * g.astype(jnp.float32)).astype(x.dtype)

def layer_norm(x, g, b, eps=1e-5):
    xf = x.astype(jnp.float32)
    mu = jnp.mean(xf, axis=-1, keepdims=True)
    xc = xf - mu
    y = xc * lax.rsqrt(jnp.mean(xc * xc, axis=-1, keepdims=True) + eps)
    return (y * g.astype(jnp.float32) + b.astype(jnp.float32)).astype(x.dtype)

def alibi_slopes(n_heads):
    return 2.0 ** (-8.0 * jnp.arange(1, n_heads + 1, dtype=jnp.float32) / n_heads)

def lambda_init_for(layer_idx):
    return 0.8 - 0.6 * math.exp(-0.3 * layer_idx)

def conformer_conv_branch(a_glu, gate, dw, dw_b, ln_g, ln_b, w_proj):
    a, b = jnp.split(a_glu, 2, axis=-1)
    u = a * jax.nn.sigmoid(b)
    u = lax.conv_general_dilated(
        u, dw[:, None, :], window_strides=(1,), padding=[(CONV_K - 1, 0)],
        dimension_numbers=("NWC", "WIO", "NWC"), feature_group_count=CONV_CH) + dw_b
    u = layer_norm(u, ln_g, ln_b)
    u = jax.nn.silu(u) * jax.nn.silu(gate)
    return u @ w_proj

def differential_attention_branch(q, k, v, gate, qn_g, kn_g, lq1, lk1, lq2, lk2,
                                  subln_g, w_proj, lambda_init):
    B, S = q.shape[0], q.shape[1]
    H, d = DIFF_HEADS, DIFF_HEAD_DIM
    nb = S // Q_BLOCK
    q = rms_norm_2(q.reshape(B, S, H, 2, d), qn_g)
    k = rms_norm_2(k.reshape(B, S, H, 2, d), kn_g)
    kt = k.transpose(0, 2, 3, 1, 4)
    vt = v.reshape(B, S, H, DIFF_V_DIM).transpose(0, 2, 1, 3)
    qb = q.reshape(B, nb, Q_BLOCK, H, 2, d).transpose(1, 0, 3, 4, 2, 5)
    lam = (jnp.exp(jnp.sum(lq1.astype(jnp.float32) * lk1.astype(jnp.float32)))
           - jnp.exp(jnp.sum(lq2.astype(jnp.float32) * lk2.astype(jnp.float32)))
           + lambda_init)
    slopes = alibi_slopes(H)
    scale = DIFF_HEAD_DIM ** -0.5
    kpos = jnp.arange(S)

    def one_block(args):
        qblk, t0 = args
        tpos = t0 + jnp.arange(Q_BLOCK)
        dist = (tpos[:, None] - kpos[None, :]).astype(jnp.float32)
        bias = -slopes[:, None, None] * dist
        s = jnp.einsum("bhmqd,bhmkd->bhmqk", qblk, kt).astype(jnp.float32) * scale
        s = s + bias[None, :, None]
        s = jnp.where(dist >= 0, s, -jnp.inf)
        p = jax.nn.softmax(s, axis=-1)
        a = (p[:, :, 0] - lam * p[:, :, 1]).astype(vt.dtype)
        return jnp.einsum("bhqk,bhkd->bhqd", a, vt)

    o = lax.map(one_block, (qb, jnp.arange(nb) * Q_BLOCK))
    o = o.transpose(1, 0, 3, 2, 4).reshape(B, S, H, DIFF_V_DIM)
    o = rms_norm_2(o, subln_g) * (1.0 - lambda_init)
    o = o.reshape(B, S, DIFF_WIDTH) * jax.nn.silu(gate)
    return o @ w_proj

def memory_cross_attention_branch(q, gate, mem_h, w_mem_kv, qn_g, kn_g, w_proj):
    B, S = q.shape[0], q.shape[1]
    M = mem_h.shape[1]
    k, v = jnp.split(mem_h @ w_mem_kv, 2, axis=-1)
    q = rms_norm_2(q.reshape(B, S, X_HEADS, X_HEAD_DIM), qn_g)
    k = rms_norm_2(k.reshape(B, M, X_HEADS, X_HEAD_DIM), kn_g)
    v = v.reshape(B, M, X_HEADS, X_HEAD_DIM)
    s = jnp.einsum("bshd,bmhd->bhsm", q, k).astype(jnp.float32) * (X_HEAD_DIM ** -0.5)
    p = jax.nn.softmax(s, axis=-1).astype(v.dtype)
    o = jnp.einsum("bhsm,bmhd->bshd", p, v).reshape(B, S, X_WIDTH) * jax.nn.silu(gate)
    return o @ w_proj

def second_inputs(seed: int = 0) -> dict:
    key = jax.random.key(seed)
    ks = jax.random.split(key, 24)
    f32 = jnp.float32
    L, D = DEPTH, D_MODEL

    def nrm(k, shape, scale):
        return jax.random.normal(k, shape, f32) * scale

    def gain(k, shape):
        return 1.0 + 0.05 * jax.random.normal(k, shape, f32)

    return {
        "x": jax.random.normal(ks[0], (BATCH, SEQ, D), f32),
        "mem": jax.random.normal(ks[1], (BATCH, MEM_LEN, D), f32),
        "norm_g": gain(ks[2], (L, D)),
        "mem_norm_g": gain(ks[3], (L, D)),
        "w_in": nrm(ks[4], (L, D, IN_COLS), D ** -0.5),
        "conv_dw": nrm(ks[5], (L, CONV_K, CONV_CH), CONV_K ** -0.5),
        "conv_dw_b": nrm(ks[6], (L, CONV_CH), 0.02),
        "conv_ln_g": gain(ks[7], (L, CONV_CH)),
        "conv_ln_b": nrm(ks[8], (L, CONV_CH), 0.02),
        "w_conv_proj": nrm(ks[9], (L, CONV_CH, D), CONV_CH ** -0.5),
        "diff_qn_g": gain(ks[10], (L, DIFF_HEAD_DIM)),
        "diff_kn_g": gain(ks[11], (L, DIFF_HEAD_DIM)),
        "lambda_q1": nrm(ks[12], (L, DIFF_HEAD_DIM), 0.1),
        "lambda_k1": nrm(ks[13], (L, DIFF_HEAD_DIM), 0.1),
        "lambda_q2": nrm(ks[14], (L, DIFF_HEAD_DIM), 0.1),
        "lambda_k2": nrm(ks[15], (L, DIFF_HEAD_DIM), 0.1),
        "diff_subln_g": gain(ks[16], (L, DIFF_V_DIM)),
        "w_diff_proj": nrm(ks[17], (L, DIFF_WIDTH, D), DIFF_WIDTH ** -0.5),
        "w_mem_kv": nrm(ks[18], (L, D, 2 * X_WIDTH), D ** -0.5),
        "x_qn_g": gain(ks[19], (L, X_HEAD_DIM)),
        "x_kn_g": gain(ks[20], (L, X_HEAD_DIM)),
        "w_x_proj": nrm(ks[21], (L, X_WIDTH, D), X_WIDTH ** -0.5),
        "w_out": nrm(ks[22], (L, D, D), D ** -0.5),
    }

def second_block(x, mem, norm_g, mem_norm_g, w_in, conv_dw, conv_dw_b, conv_ln_g, conv_ln_b,
              w_conv_proj, diff_qn_g, diff_kn_g, lambda_q1, lambda_k1, lambda_q2, lambda_k2,
              diff_subln_g, w_diff_proj, w_mem_kv, x_qn_g, x_kn_g, w_x_proj, w_out):
    B, S, D = x.shape
    for l in range(DEPTH):
        h = rms_norm_2(x, norm_g[l])
        mem_h = rms_norm_2(mem, mem_norm_g[l])
        (c_glu, c_gate, d_q, d_k, d_v, d_gate, x_q, x_gate, merge) = jnp.split(
            h @ w_in[l], IN_SPLITS, axis=-1)
        y_conv = conformer_conv_branch(c_glu, c_gate, conv_dw[l], conv_dw_b[l],
                                       conv_ln_g[l], conv_ln_b[l], w_conv_proj[l])
        y_diff = differential_attention_branch(
            d_q, d_k, d_v, d_gate, diff_qn_g[l], diff_kn_g[l], lambda_q1[l], lambda_k1[l],
            lambda_q2[l], lambda_k2[l], diff_subln_g[l], w_diff_proj[l], lambda_init_for(l))
        y_mem = memory_cross_attention_branch(x_q, x_gate, mem_h, w_mem_kv[l],
                                              x_qn_g[l], x_kn_g[l], w_x_proj[l])
        g = jax.nn.sigmoid(merge.reshape(B, S, N_BRANCH, D))
        y = g[:, :, 0] * y_conv + g[:, :, 1] * y_diff + g[:, :, 2] * y_mem
        x = x + y @ w_out[l]
    return x


def setup_inputs(seed=0):
    out = dict(first_inputs(seed))
    for name, value in second_inputs(seed + 1).items():
        if name != "x":
            out[name + "_2"] = value
    return out


def reference(
    x, c, positions, w_ada, b_ada, g_pre, w_in, b_fgate, sinks, w_out, g_post, mem_2, norm_g_2,
    mem_norm_g_2, w_in_2, conv_dw_2, conv_dw_b_2, conv_ln_g_2, conv_ln_b_2, w_conv_proj_2,
    diff_qn_g_2, diff_kn_g_2, lambda_q1_2, lambda_k1_2, lambda_q2_2, lambda_k2_2,
    diff_subln_g_2, w_diff_proj_2, w_mem_kv_2, x_qn_g_2, x_kn_g_2, w_x_proj_2, w_out_2,
):
    x = first_block(
        x, c, positions, w_ada, b_ada, g_pre, w_in, b_fgate, sinks, w_out, g_post,
    )
    return second_block(
        x, mem_2, norm_g_2, mem_norm_g_2, w_in_2, conv_dw_2, conv_dw_b_2, conv_ln_g_2,
        conv_ln_b_2, w_conv_proj_2, diff_qn_g_2, diff_kn_g_2, lambda_q1_2, lambda_k1_2,
        lambda_q2_2, lambda_k2_2, diff_subln_g_2, w_diff_proj_2, w_mem_kv_2, x_qn_g_2, x_kn_g_2,
        w_x_proj_2, w_out_2,
    )


_drawn_inputs = setup_inputs


def setup_inputs(seed=0):
    import zlib

    import numpy as np

    out = dict(_drawn_inputs(seed))
    spreads = {}
    factors = {'sinks': 8.0,
     'mem_norm_g_2': 8.0,
     'conv_dw_b_2': 8.0,
     'conv_ln_g_2': 15.223,
     'conv_ln_b_2': 37.568,
     'diff_qn_g_2': 6.772,
     'diff_kn_g_2': 5.837,
     'lambda_q2_2': 8.0,
     'lambda_k2_2': 8.0,
     'diff_subln_g_2': 12.602,
     'x_qn_g_2': 8.0,
     'x_kn_g_2': 8.0}
    for name, (base, spread) in spreads.items():
        noise = np.random.default_rng([zlib.crc32(name.encode()), seed]).standard_normal(out[name].shape)
        drawn = base * np.exp(spread * noise) if base else spread * noise
        out[name] = __import__('jax').numpy.asarray(drawn.astype(out[name].dtype))
    for name, factor in factors.items():
        out[name] = (out[name] * factor).astype(out[name].dtype)
    return out
```

```python
from contextlib import ExitStack

import numpy as np

import concourse.bass as bass
from concourse import mybir

F32 = mybir.dt.float32
F32R = mybir.dt.float32r
F16 = mybir.dt.float16
BF16 = mybir.dt.bfloat16
I32 = mybir.dt.int32
ACT = mybir.ActivationFunctionType
ALU = mybir.AluOpType
AX = mybir.AxisListType.X

P = 128
D = 1024
S = 512
T = S // P
C = D // P
HD = 64
MEM = 256
TAPS = 31
PAD = TAPS - 1
MASKED = -1.0e30
MAGIC = 12582912.0
TWO_PI_A, TWO_PI_B, TWO_PI_C = 6.28125, 0.0019350051879882812, 3.0199159819e-07
PI = 3.1415925
LAMBDA_INIT = 0.8 - 0.6

K_IDENT, K_BLOCKS, K_ONES, K_ROT, K_PREV, K_CAUSAL, K_DIST, K_FREQ = 0, 128, 256, 384, 512, 640, 768, 1280
K_COLS = 1281
VEC_ROWS = [("c", 8), ("b_ada", 16), ("g_pre", 8), ("norm_g", 8), ("mem_g", 8), ("dw_b", 8), ("ln_g", 8),
            ("ln_b", 8), ("dqn", 1), ("dkn", 1), ("subln", 1), ("xqn", 2), ("xkn", 2)]
VEC = {}
_at = 0
for _name, _count in VEC_ROWS:
    VEC[_name] = (_at, _count)
    _at += _count
NVEC = 96

CHUNKS = [("mk", j) for j in range(8)] + [("mv", j) for j in range(8)]
CHUNKS += [("fa", 0), ("qa", 0)] + [("va", j) for j in range(4)] + [("ka", 0)]
for _c in range(3):
    CHUNKS += [("qa", _c + 1), ("ka", _c + 1), ("za", _c), ("zb", _c)]
CHUNKS += [("kb", 0), ("vb", 0), ("za", 3), ("zb", 3), ("qb", 0), ("qb", 1), ("qb", 2), ("qb", 3)]
CHUNKS += [("wo", j) for j in range(8)] + [("dv", j) for j in range(8)] + [("dq", 0), ("dk", 0)]
for _j in range(8):
    if _j < 7:
        CHUNKS += [("dq", _j + 1), ("dk", _j + 1)]
    CHUNKS += [("gb", _j), ("ga", _j), ("dg", _j)]


def _branch(b):
    out = [("m" + b, 0), ("m" + b, 1)]
    for j in range(8):
        out.append(("p" + b, j))
        if j + 2 < 8:
            out.append(("m" + b, j + 2))
    return out


CHUNKS += _branch("d") + [("xq", 0), ("xq", 1)]
for _h in range(4):
    if _h < 3:
        CHUNKS += [("xq", 2 * _h + 2), ("xq", 2 * _h + 3)]
    CHUNKS += [("xg", 2 * _h), ("xg", 2 * _h + 1)]
CHUNKS += _branch("x") + [("cg", j) for j in range(8)] + _branch("c") + [("w2", j) for j in range(8)]
NCH = {name: n for n, name in enumerate(CHUNKS)}
PAIRED = ("mv", "va", "wo", "dv", "w2")
RAWS, SPLITS = 4, 4
NADA = 24
RAW = CHUNKS[:4]
for _i in range(6):
    RAW = RAW + [("ada", 4 * _i + j) for j in range(4)] + CHUNKS[4 + 2 * _i:6 + 2 * _i]
RAW = RAW + CHUNKS[16:]
NRAW = {name: n for n, name in enumerate(RAW)}


def plan_slots():
    slot, before, last, at = {}, {}, {}, 0
    for name in CHUNKS:
        if name[0] in PAIRED and name[1] % 2 == 0 and at % 2:
            at += 1
        slot[name] = at % SPLITS
        before[name] = last.get(at % SPLITS)
        last[at % SPLITS] = name
        at += 1
    return slot, before


SLOT, BEFORE = plan_slots()


def constants():
    k = np.zeros((P, K_COLS), np.float32)
    i = np.arange(P)
    k[:, K_IDENT:K_IDENT + P] = np.eye(P)
    k[:, K_BLOCKS:K_BLOCKS + P] = (i[:, None] // HD) == (i[None, :] // HD)
    k[:, K_ONES:K_ONES + P] = 1.0
    for o in range(P):
        if o % HD < HD // 2:
            k[o + HD // 2, K_ROT + o] = -1.0
        else:
            k[o - HD // 2, K_ROT + o] = 1.0
    k[:, K_CAUSAL:K_CAUSAL + P] = np.where(i[None, :] <= i[:, None], 0.0, MASKED)
    k[:, K_PREV:K_PREV + P] = np.where(i[None, :] > i[:, None], 0.0, MASKED)
    j = np.arange(S)
    k[:, K_DIST:K_DIST + S] = (j[None, :] - (S - P)) - i[:, None]
    k[:, K_FREQ] = (10000.0 ** (-(i % (HD // 2)).astype(np.float64) / (HD // 2))).astype(np.float32)
    return k


class Banks:

    def __init__(self, filled, emptied):
        self.filled, self.emptied = filled, emptied
        self.uses = [0] * len(filled)
        self.where = {}

    def open(self, pe, bank, key):
        self.uses[bank] += 1
        self.where[key] = (bank, self.uses[bank])
        if self.uses[bank] > 1:
            pe.wait_ge(self.emptied[bank], self.uses[bank] - 1)

    def close(self, ins, key):
        ins.then_inc(self.filled[self.where[key][0]], 1)

    def wait_full(self, eng, key):
        bank, n = self.where[key]
        eng.wait_ge(self.filled[bank], n)

    def empty(self, ins, key):
        ins.then_inc(self.emptied[self.where[key][0]], 1)

    def wait_empty(self, eng, key):
        bank, n = self.where[key]
        eng.wait_ge(self.emptied[bank], n)


def build(nc, t, out):
    ctx = ExitStack()
    with ctx:
        def sb(name, shape, dt=F32):
            return ctx.enter_context(nc.sbuf_tensor(name, shape, dt))

        def shared(*groups):
            got = []
            for n, group in enumerate(groups):
                with ExitStack() as own:
                    for spec in group:
                        if n < len(groups) - 1:
                            got.append(own.enter_context(nc.sbuf_tensor(*spec)))
                        else:
                            got.append(sb(*spec))
            return got

        def sem(name):
            return ctx.enter_context(nc.semaphore(name))

        raw = sb("raw", [P, RAWS, C, P])
        wh = sb("wh", [P, SPLITS, C, P], F32R)
        wl = sb("wl", [P, SPLITS, C, P], F32R)
        hh = sb("hh", [P, C, S], F32R)
        hl = sb("hl", [P, C, S], F32R)
        acc_odd, oh = shared([("acc_odd", [P, 3 * D], F32)], [("oh", [P, C, S], F32R)])
        memx, xn, ol = shared([("memx", [P, 2, D], F32)], [("xn", [P, T, D], F32)], [("ol", [P, C, S], F32R)])
        va, vb, kvm, ytok, dv, x1r = shared([("va", [P, T, S], F32), ("vb", [P, T, P], F32)],
                                            [("kvm", [P, 2, 2 * D], F32)], [("ytok", [P, T, D], F32)],
                                            [("dv", [P, T, D], F32)], [("x1r", [P, T, D], F32)])
        km = kvm[:, 0, :].rearrange("p (c n) -> p c n", n=MEM)
        vm = kvm[:, 1, :].rearrange("p (t n) -> p t n", n=D)
        acc_even, bgate, negcum, sel, gate, u = shared(
            [("acc_even", [P, 3 * D], F32), ("bgate", [P, D], F32)],
            [("negcum", [P, 2, S], F32R), ("sel", [P, 8, P], F32R), ("gate", [P, D], F32)],
            [("u", [P, C, PAD + S], F32)])
        cos, sin, gzb, rot, x, y = shared([("cos", [P, S], F32), ("sin", [P, S], F32), ("gzb", [P, 4, S], F32),
                                           ("rot", [P, P], F32)], [("x", [P, T, D], F32)], [("y", [P, C, S], F32)])
        ident = sb("ident", [P, P])
        blocks = sb("blocks", [P, P])
        ones = sb("ones", [P, P])
        masks = sb("masks", [P, 2, P], BF16)
        ident_b = sb("ident_b", [P, P], BF16)
        dist = sb("dist", [P, S], F16)
        slopes = sb("slopes", [P, 8, P], F16)
        vec = sb("vec", [P, NVEC])
        taps = sb("taps", [P, TAPS * C])
        sc = sb("sc", [P, 112])
        rsm, prob = shared([("rsm", [P, 2 * S], F32)], [("prob", [P, 3, S], F32)])
        kload, gp, pth = shared([("kload", [P, K_COLS - K_PREV], F32), ("gp", [P, D], F32)], [("pth", [P, T, S], F32R)])
        vrows, cumt, ptl = shared([("vrows", [P, 3, P], F32)], [("cumt", [P, 4, S], F32)], [("ptl", [P, T, S], F32R)])
        th = sb("th", [P, S])
        sq = sb("sq", [P, S])
        rs = sb("rs", [P, S])
        qf = sb("qf", [P, 2, S])
        qk = sb("qk", [P, 4, S], F32R)
        qh, ql, kh, kl = (qk[:, n, :] for n in range(4))
        gj = sb("gj", [P, S])
        mx = sb("mx", [P, S])
        pos, lam4, ca, xk = shared([("pos", [P, S], I32), ("lam4", [P, 4, HD], F32)], [("ca", [P, 2, S], F32)],
                                   [("xk", [P, 2, 2, MEM], F32R)])
        vv = sb("vv", [P, 2, T, P], F32R)
        vh, vl = vv[:, 0], vv[:, 1]
        stat = sb("stat", [P, 3, 16])
        MEM_SS, X_SS, Y_SS, X1_SS = sc[:, 0:2], sc[:, 2:6], sc[:, 6:10], sc[:, 10:14]
        freq, nlam, lsum = sc[:, 14:15], sc[:, 15:16], sc[:, 16:18]
        tc_, cc_ = sc[:, 18:26], sc[:, 26:34]
        modc, scale_a = sc[:, 34:50], sc[:, 50:58]
        sinks, nsinks, fbias = sc[:, 58:66], sc[:, 66:74], sc[0:8, 74:75]
        esink = sc[:, 80:96]
        ps = [ctx.enter_context(nc.psum_tensor(f"bank{n}", [P, S], F32)) for n in range(8)]

        mem_scratch = nc.dram_tensor("mem_scratch", [P, 2, 2 * D], F32).ap()
        x1_scratch = nc.dram_tensor("x1_scratch", [P, T, D], F32).ap()

        banks = Banks([sem(f"filled{n}") for n in range(8)], [sem(f"emptied{n}") for n in range(8)])
        raw_loaded = [sem(f"raw_loaded{n}") for n in range(RAWS)]
        names = """raw_used w_hi w_lo const_in rows_in mem_in x_in bcast_in kvm_out kvm_in x1_out x1_in x_again out_sem
            rot_in rows_clear const_done vec_done ada_step dve_step act_step lam_done mod_done h_hi h_lo o_hi o_lo q_hi q_lo
            pt_hi v_hi v_lo memk_hi memk_lo tanhed sumsq squared ms_done rms_done nk_done xn_done negmax expd
            prob_ready logs cum_hi cum_done cum_act cum_dve rope_in rope_out roped qn_done of_copied kvm_ready
            mixed x1_done conv_done ln_act lnx ln_centred ln_scaled ln_t y_sum yhi ylo c_tanh"""
        names = names.split()
        sems = {n: sem(n) for n in names}
        s = type("Signals", (), sems)

        def v(name, j=0):
            return vec[:, VEC[name][0] + j:VEC[name][0] + j + 1]

        block = ctx.enter_context(nc.Block())

        def rows(w):
            return w.rearrange("(c p) n -> p c n", p=P)

        w_in, w_in_2, w_mem = rows(t["w_in"][0]), rows(t["w_in_2"][0]), rows(t["w_mem_kv_2"][0])
        w_ada, w_out_2 = rows(t["w_ada"][0]), rows(t["w_out_2"][0])
        projs = {"pd": rows(t["w_diff_proj_2"][0]), "px": rows(t["w_x_proj_2"][0]), "pc": rows(t["w_conv_proj_2"][0])}
        first = {"qa": 0, "ka": 512, "va": 1024, "fa": 1536, "za": 1544, "kb": 2568, "vb": 2696}
        second = {"ga": 0, "gb": 1024, "cg": 2048, "dq": 3072, "dk": 4096, "dv": 5120, "dg": 6144, "xq": 7168,
                  "xg": 8192, "mc": 9216, "md": 10240, "mx": 11264}

        def pieces(name):
            kind, j = name
            whole = lambda dst: dst
            if kind in ("mk", "mv"):
                at = j * P + (D if kind == "mv" else 0)
                return [(whole, w_mem[:, :, at:at + P])]
            if kind == "ada":
                return [(whole, w_ada[:, :, j * P:j * P + P])]
            if kind in projs:
                return [(whole, projs[kind][:, :, j * P:j * P + P])]
            if kind == "w2":
                return [(whole, w_out_2[:, :, j * P:j * P + P])]
            if kind in ("qb", "zb"):
                at = (2056 if kind == "qb" else 2824) + j * HD
                return [(lambda dst, i=i: dst[:, :, i * HD:i * HD + HD],
                         w_in[:, :, at + 256 * i:at + 256 * i + HD]) for i in range(2)]
            if kind == "wo":
                cols = slice(j * P, j * P + P)
                wo = t["w_out"][0]
                halves = [(lambda dst, i=i: dst[i * HD:i * HD + HD, 4:8, :],
                           wo[512 + 256 * i:768 + 256 * i, cols].rearrange("(c p) n -> p c n", p=HD)) for i in range(2)]
                return [(lambda dst: dst[:, 0:4, :], rows(wo[0:512, :])[:, :, cols])] + halves
            if kind in first:
                return [(whole, w_in[:, :, first[kind] + j * P:first[kind] + j * P + P])]
            return [(whole, w_in_2[:, :, second[kind] + j * P:second[kind] + j * P + P])]

        raw_count = [0] * RAWS
        raw_at = {}
        for n, name in enumerate(RAW):
            raw_count[n % RAWS] += 16 * len(pieces(name))
            raw_at[name] = (n % RAWS, raw_count[n % RAWS])

        def wait_raw(eng, name):
            slot, count = raw_at[name]
            eng.wait_ge(raw_loaded[slot], count)

        done_by = {}

        @block.tensor
        def _(pe):
            proj_bank = [0]

            def next_bank(n=2):
                proj_bank[0] += 1
                return proj_bank[0] % n

            def three(o, a, b, start, stop, **kw):
                pe.matmul(o, a[0], b[1], start=start, stop=False, **kw)
                pe.matmul(o, a[1], b[0], start=False, stop=False, **kw)
                return pe.matmul(o, a[0], b[0], start=False, stop=stop, **kw)

            def chunk(name, act, nb=2, bank=None, fill=None):
                pe.wait_ge(s.raw_used, NRAW[name] + 1)
                b = next_bank(nb) if bank is None else bank
                if fill is None:
                    banks.open(pe, b, name)
                o = ps[b][:] if fill is None else fill
                w = SLOT[name]
                for c in range(C):
                    ins = three(o, (wh[:, w, c, :], wl[:, w, c, :]), (act[0][:, c], act[1][:, c]), c == 0, c == C - 1)
                if fill is None:
                    banks.close(ins, name)
                    done_by[name] = name
                return ins

            H = (hh, hl)
            O = (oh, ol)

            def by_token(kind, g, act, tiles, nb=2, width=256):
                name = (kind, 2 * g)
                pe.wait_ge(s.raw_used, NRAW[(kind, 2 * g + 1)] + 1)
                w = SLOT[name]
                for pair in range(tiles // 2):
                    key = (kind, g, pair)
                    b = next_bank(nb)
                    banks.open(pe, b, key)
                    for tt in range(2):
                        tok = slice((2 * pair + tt) * P, (2 * pair + tt + 1) * P)
                        for c in range(C):
                            ins = three(ps[b][:, 256 * tt:256 * tt + 256], (act[0][:, c, tok], act[1][:, c, tok]),
                                        (wh[:, w:w + 2, c, :], wl[:, w:w + 2, c, :]), c == 0, c == C - 1)
                    banks.close(ins, key)
                done_by[name] = done_by[(kind, 2 * g + 1)] = key

            def total(key, squares, ones_, n=S, bank=7):
                banks.open(pe, bank, key)
                for i, x_ in enumerate(squares):
                    ins = pe.matmul(ps[bank][:, 0:n], ones_[:], x_, start=i == 0, stop=i == len(squares) - 1)
                banks.close(ins, key)

            pe.wait_ge(s.const_in, 16 * 4)
            pe.wait_ge(s.rows_in, 16 * 16)
            banks.open(pe, 7, "vec")
            banks.close(pe.transpose(ps[7][:, 0:NVEC], vrows[0:NVEC, 0, :], ident[0:NVEC, 0:NVEC]), "vec")
            banks.open(pe, 6, "taps")
            for i in range(2):
                ins = pe.transpose(ps[6][:, 124 * i:124 * i + 124], vrows[0:124, 1 + i, :], ident[0:124, 0:124])
            banks.close(ins, "taps")

            pe.wait_ge(s.nk_done, 2)
            for g in range(4):
                banks.open(pe, 2 + g % 2, ("memT", g))
                for cc in range(2):
                    for tt in range(2):
                        ins = pe.transpose(ps[2 + g % 2][:, (2 * cc + tt) * P:(2 * cc + tt + 1) * P],
                                           memx[:, tt, (2 * g + cc) * P:(2 * g + cc + 1) * P], ident[:])
                banks.close(ins, ("memT", g))
            MT = (hh[:, :, 0:MEM], hl[:, :, 0:MEM])
            for g in (2, 3):
                banks.wait_empty(pe, ("memT", g))
            for h in range(4):
                b = next_bank()
                banks.open(pe, b, ("mk", h, "k"))
                for i in range(2):
                    ins = chunk(("mk", 2 * h + i), MT, bank=b, fill=ps[b][:, 256 * i:256 * i + 256])
                    done_by[("mk", 2 * h + i)] = ("mk", h, "k")
                banks.close(ins, ("mk", h, "k"))
                if h > 0:
                    pe.wait_ge(s.squared, h)
                    total(("mks", h - 1), [sq[:, 0:256], sq[:, 256:512]], ones, 256)
            for g in range(4):
                by_token("mv", g, MT, 2)
                if g == 0:
                    pe.wait_ge(s.squared, 4)
                    total(("mks", 3), [sq[:, 0:256], sq[:, 256:512]], ones, 256)

            pe.wait_ge(s.raw_used, NRAW[("ada", NADA - 1)] + 1)
            banks.open(pe, 7, "mod")
            for j in range(16):
                for i, a in enumerate((acc_even, acc_odd)):
                    ins = pe.matmul(ps[7][:, j:j + 1], a[:, j * P:j * P + P], ones[:, 0:1], start=i == 0, stop=i == 1)
            banks.close(ins, "mod")
            for k in range(2):
                banks.open(pe, 4 + k, ("gate", k))
                for i, a in enumerate((acc_even, acc_odd)):
                    ins = pe.matmul(ps[4 + k][:], ones[:], a[:, 2 * D + S * k:2 * D + S * k + S], start=i == 0, stop=i == 1)
                banks.close(ins, ("gate", k))

            def to_features(src, who):
                for c in range(C):
                    b = 2 + c % 2
                    banks.open(pe, b, (who, c))
                    for tt in range(T):
                        ins = pe.transpose(ps[b][:, tt * P:tt * P + P], src[:, tt, c * P:c * P + P], ident[:])
                    banks.close(ins, (who, c))

            pe.wait_ge(s.xn_done, 4)
            to_features(xn, "xT")

            pe.wait_ge(s.h_lo, 8)
            chunk(("fa", 0), H)
            chunk(("qa", 0), H)
            for g in range(2):
                by_token("va", g, H, T)
            chunk(("ka", 0), H)

            def fox_scores(h, tt):
                u_ = 4 * h + tt
                w = P * (tt + 1)
                b = 2 + u_ % 4
                half = slice(HD * (h % 2), HD * (h % 2) + HD)
                q_ = slice(tt * P, tt * P + P)
                if tt == 0 and h % 2 == 0:
                    pe.wait_ge(s.q_lo, 2 * (h // 2) + 2)
                if u_ == 0:
                    pe.wait_ge(s.cum_done, 1)
                    pe.wait_ge(s.const_done, 1)
                banks.open(pe, b, ("S", u_))
                o = ps[b][:, 0:w]
                three(o, (qh[half, q_], ql[half, q_]), (kh[half, 0:w], kl[half, 0:w]), True, False)
                pick = sel[0:8, h, :]
                pe.matmul(o, pick, negcum[0:8, 1, 0:w], start=False, stop=False)
                pe.matmul(o, pick, negcum[0:8, 0, 0:w], start=False, stop=True)
                ins = pe.matmul(ps[b][:, w - P:w], ident_b[:], masks[:, 1, :], start=False, stop=True, skip_group_check=True)
                banks.close(ins, ("S", u_))

            def turn(u_, key, src_blocks):
                pe.wait_ge(s.prob_ready, u_ + 1)
                banks.open(pe, 6, key)
                for n, blk in enumerate(src_blocks):
                    ins = pe.transpose(ps[6][:, n * P:n * P + P], blk, ident[:])
                banks.close(ins, key)

            def values_causal(key, v_count, last_pt):
                banks.wait_empty(pe, last_pt)
                pe.wait_ge(s.v_lo, v_count)
                banks.open(pe, 7, key)
                for kb in range(T):
                    ins = three(ps[7][:, kb * P:S], (vh[:, kb, :], vl[:, kb, :]),
                                (pth[:, kb, kb * P:S], ptl[:, kb, kb * P:S]), kb == 0, True, skip_group_check=True)
                banks.close(ins, key)

            for c in range(4):
                fill = [("qa", c + 1), ("ka", c + 1), ("za", c), ("zb", c)] if c < 3 else \
                    [("kb", 0), ("vb", 0), ("za", 3), ("zb", 3)]
                for k in range(8 + 3):
                    if k < 8:
                        fox_scores(2 * c + k // 4, k % 4)
                    if k % 2 == 1 and k < 8:
                        name = fill[k // 2]
                        if name[0] == "vb":
                            pe.wait_ge(s.raw_used, NRAW[name] + 1)
                            b = next_bank()
                            banks.open(pe, b, name)
                            w = SLOT[name]
                            for tt in range(T):
                                tok = slice(tt * P, tt * P + P)
                                for cc in range(C):
                                    ins = three(ps[b][:, tok], (hh[:, cc, tok], hl[:, cc, tok]),
                                                (wh[:, w, cc, :], wl[:, w, cc, :]), cc == 0, cc == C - 1)
                            banks.close(ins, name)
                            done_by[name] = name
                        else:
                            chunk(name, H)
                    if 0 <= k - 2 < 8:
                        u_ = 8 * c + k - 2
                        turn(u_, ("PT", u_), [prob[:, u_ % 2, i * P:i * P + P] for i in range(u_ % 4 + 1)])
                    if k >= 6 and (k - 3) % 4 == 3:
                        h = 2 * c + (k - 3) // 4
                        values_causal(("PO", h), c + 1, ("PT", 4 * h + 3))

            def rotate(key):
                banks.wait_empty(pe, key)
                pe.wait_ge(s.rot_in, 16)
                banks.open(pe, 7, ("rot",) + key)
                banks.close(pe.matmul(ps[7][:], rot[:], qf[:, 0, :], start=True, stop=True), ("rot",) + key)

            rotate(("kb", 0))
            chunk(("qb", 0), H)
            rotate(("qb", 0))

            def swa_scores(n, i, g, tt):
                u_ = 32 + n
                b = 2 + u_ % 4
                half = slice(HD * g, HD * g + HD)
                q_ = slice(tt * P, tt * P + P)
                lo = max(tt - 1, 0) * P
                w = P if tt == 0 else 2 * P
                if n % 8 == 0:
                    pe.wait_ge(s.q_lo, 8 + i + 2)
                banks.open(pe, b, ("S", u_))
                o = ps[b][:, 2 * P - w:2 * P]
                three(o, (qh[half, q_], ql[half, q_]), (kh[half, lo:lo + w], kl[half, lo:lo + w]), True, False)
                m = masks[:, 2 - w // P:2, :]
                ins = pe.matmul(o, ident_b[:], m, start=False, stop=True)
                banks.close(ins, ("S", u_))

            for i in range(4):
                for k in range(8 + 3):
                    if k < 8:
                        swa_scores(8 * i + k, i, k // 4, k % 4)
                    if k == 3 and i < 3:
                        chunk(("qb", i + 1), H)
                    if 0 <= k - 2 < 8:
                        n = 8 * i + k - 2
                        u_ = 32 + n
                        src = [prob[:, u_ % 2, P * j:P * j + P] for j in (range(2) if n % 4 else [1])]
                        turn(u_, ("PT", u_), src)
                    if k >= 6 and (k - 3) % 4 == 3:
                        h = 8 + 2 * i + (k - 3) // 4
                        banks.wait_empty(pe, ("PT", 4 * h + 3))
                        pe.wait_ge(s.v_lo, 5)
                        banks.open(pe, 7, ("PO", h))
                        for kb in range(T):
                            w = P if kb == T - 1 else 2 * P
                            ins = three(ps[7][:, kb * P:kb * P + w], (vh[:, kb, :], vl[:, kb, :]),
                                        (pth[:, kb, kb * P:kb * P + w], ptl[:, kb, kb * P:kb * P + w]),
                                        kb == 0, True, skip_group_check=True)
                        banks.close(ins, ("PO", h))
                if i < 3:
                    rotate(("qb", i + 1))

            pe.wait_ge(s.o_lo, 8)
            for g in range(4):
                by_token("wo", g, O, T, 4)

            pe.wait_ge(s.xn_done, 8)
            to_features(ytok, "x1T")
            for c in (6, 7):
                banks.wait_empty(pe, ("x1T", c))
            for g in range(4):
                by_token("dv", g, H, T)
            chunk(("dq", 0), H)
            chunk(("dk", 0), H)
            for i in range(2):
                pe.wait_ge(s.squared, 4 + 1 + i)
                total(("dns", i), [sq[:]], blocks)

            def diff_scores(j, tt):
                u_ = 4 * j + tt
                w = P * (tt + 1)
                q_ = slice(tt * P, tt * P + P)
                if tt == 0:
                    pe.wait_ge(s.q_lo, 13 + 2 * j + 2)
                for m in range(2):
                    b = 2 + 2 * (u_ % 2) + m
                    half = slice(HD * m, HD * m + HD)
                    banks.open(pe, b, ("D", u_, m))
                    o = ps[b][:, 0:w]
                    three(o, (qh[half, q_], ql[half, q_]), (kh[half, 0:w], kl[half, 0:w]), True, False)
                    pe.matmul(o, slopes[:, j, :], dist[:, S - w:S], start=False, stop=True)
                    ins = pe.matmul(ps[b][:, w - P:w], ident_b[:], masks[:, 1, :], start=False, stop=True,
                                    skip_group_check=True)
                    banks.close(ins, ("D", u_, m))

            def diff_turn(u_):
                turn(64 + u_, ("DT", u_), [prob[:, u_ % 2, i * P:i * P + P] for i in range(u_ % 4 + 1)])

            def diff_values(j):
                values_causal(("DO", j), 6 + j, ("DT", 4 * j + 3))

            def subln(j):
                pe.wait_ge(s.of_copied, j + 1)
                total(("sub", j), [sq[:]], ones)

            for j in range(8):
                for tt in range(4):
                    if tt == 0 and j < 7:
                        chunk(("dq", j + 1), H)
                    if tt == 1 and j < 7:
                        chunk(("dk", j + 1), H)
                    if tt == 2:
                        chunk(("gb", j), H)
                        chunk(("ga", j), H)
                    if tt == 3:
                        chunk(("dg", j), H)
                    diff_scores(j, tt)
                    if 4 * j + tt > 0:
                        diff_turn(4 * j + tt - 1)
                    if tt == 0 and j > 0:
                        diff_values(j - 1)
                    if tt == 1 and j > 0:
                        subln(j - 1)
                    if tt in (2, 3) and j < 7:
                        pe.wait_ge(s.squared, 4 + 2 + 2 * j + tt - 1)
                        total(("dns", 2 * j + tt), [sq[:]], blocks)
            diff_turn(31)
            diff_values(7)

            def branch(b, o_count, first_=None):
                chunk(("m" + b, 0), H, 4)
                if first_:
                    first_()
                chunk(("m" + b, 1), H, 4)
                for j in range(8):
                    if j == 0:
                        pe.wait_ge(s.o_lo, o_count)
                    chunk(("p" + b, j), O, 4)
                    if j + 2 < 8:
                        chunk(("m" + b, j + 2), H, 4)

            branch("d", 16, lambda: subln(7))

            for i in range(2):
                chunk(("xq", i), H)

            def xq_sums(h):
                pe.wait_ge(s.squared, 4 + 16 + h + 1)
                total(("xns", h), [sq[:], rs[:]], ones)

            def x_scores(h, pr):
                u_ = 2 * h + pr
                b = 2 + u_ % 4
                if pr == 0:
                    pe.wait_ge(s.q_lo, 29 + 2 * h + 2)
                    pe.wait_ge(s.memk_lo, h + 1)
                banks.open(pe, b, ("X", u_))
                for tt in range(2):
                    q_ = slice((2 * pr + tt) * P, (2 * pr + tt + 1) * P)
                    o = ps[b][:, 256 * tt:256 * tt + 256]
                    three(o, (qh[:, q_], ql[:, q_]), (xk[:, 0, 0, :], xk[:, 1, 0, :]), True, False)
                    ins = three(o, (kh[:, q_], kl[:, q_]), (xk[:, 0, 1, :], xk[:, 1, 1, :]), False, True)
                banks.close(ins, ("X", u_))

            def x_turn(u_):
                src = [prob[:, u_ % 2, 256 * tt + kb * P:256 * tt + kb * P + P] for kb in range(2) for tt in range(2)]
                turn(96 + u_, ("XT", u_), src)

            def x_values(h):
                banks.wait_empty(pe, ("XT", 2 * h + 1))
                pe.wait_ge(s.v_lo, 14 + h)
                for i in range(2):
                    banks.open(pe, 7, ("XO", h, i))
                    for kb in range(2):
                        ins = three(ps[7][:], (vh[:, 2 * kb + i, :], vl[:, 2 * kb + i, :]),
                                    (pth[:, kb, :], ptl[:, kb, :]), kb == 0, kb == 1)
                    banks.close(ins, ("XO", h, i))

            xq_sums(0)
            for h in range(4):
                for pr in range(2):
                    if pr == 0 and h < 3:
                        for i in range(2):
                            chunk(("xq", 2 * h + 2 + i), H)
                    if pr == 1:
                        for i in range(2):
                            chunk(("xg", 2 * h + i), H)
                    x_scores(h, pr)
                    if 2 * h + pr > 0:
                        x_turn(2 * h + pr - 1)
                    if pr == 0 and h > 0:
                        x_values(h - 1)
                    if pr == 1 and h < 3:
                        xq_sums(h + 1)
            x_turn(7)
            x_values(3)
            branch("x", 24)

            pe.wait_ge(s.conv_done, 8)
            total("ln_sum", [u[:, j, PAD:] for j in range(C)], ones)
            chunk(("cg", 0), H)
            banks.open(pe, 7, "ln_var")
            for j in range(C):
                pe.wait_ge(s.ln_act, j + 1)
                ins = pe.matmul(ps[7][:], ones[:], (sq if j % 2 == 0 else mx)[:], start=j == 0, stop=j == C - 1)
                if j < C - 1:
                    ins.then_inc(s.lnx, 1)
            banks.close(ins, "ln_var")
            for j in range(1, 8):
                chunk(("cg", j), H)
            branch("c", 32)

            pe.wait_ge(s.ylo, 8)
            for g in range(4):
                by_token("w2", g, H, T, 4)

        @block.sync
        def _(sp):
            for n, name in enumerate(RAW):
                if n >= RAWS:
                    sp.wait_ge(s.raw_used, n - RAWS + 1)
                slot = n % RAWS
                for where, src in pieces(name):
                    sp.dma_start(where(raw[:, slot]), src).then_inc(raw_loaded[slot], 16)

        @block.gpsimd
        def _(pool):
            pool.dma_start(ident[:], t["consts"][:, K_IDENT:K_IDENT + P]).then_inc(s.const_in, 16)
            pool.dma_start(kload[:], t["consts"][:, K_PREV:K_COLS]).then_inc(s.const_in, 16)
            pool.dma_start(memx[:], t["mem_2"][0].rearrange("(t p) d -> p t d", p=P)).then_inc(s.mem_in, 16)
            pool.memset(vrows[:], 0.0).then_inc(s.rows_clear, 1)
            pool.wait_ge(s.rows_clear, 1)
            vectors = [("c", t["c"]), ("b_ada", t["b_ada"][:, 0:2 * D]), ("g_pre", t["g_pre"]),
                       ("norm_g", t["norm_g_2"]), ("mem_g", t["mem_norm_g_2"]), ("dw_b", t["conv_dw_b_2"]),
                       ("ln_g", t["conv_ln_g_2"]), ("ln_b", t["conv_ln_b_2"]), ("subln", t["diff_subln_g_2"]),
                       ("xqn", t["x_qn_g_2"]), ("xkn", t["x_kn_g_2"])]
            for name, src in vectors:
                a, n = VEC[name]
                pool.dma_start(vrows[a:a + n, 0, :], src.rearrange("a (r p) -> (a r) p", p=P)).then_inc(s.rows_in, 16)
            for name, src in (("dqn", t["diff_qn_g_2"]), ("dkn", t["diff_kn_g_2"])):
                for i in range(2):
                    pool.dma_start(vrows[VEC[name][0]:VEC[name][0] + 1, 0, HD * i:HD * i + HD], src).then_inc(s.rows_in, 16)
            dw = t["conv_dw_2"][0].rearrange("k (j p) -> (k j) p", p=P)
            pool.dma_start(vrows[0:124, 1:3, :], dw.rearrange("(a r) p -> r a p", a=2)).then_inc(s.rows_in, 16)
            pool.dma_start(blocks[:], t["consts"][:, K_BLOCKS:K_BLOCKS + P]).then_inc(s.const_in, 16)
            pool.dma_start(ones[:], t["consts"][:, K_ONES:K_ONES + P]).then_inc(s.const_in, 16)
            pool.dma_start(x[:], t["x"][0].rearrange("(t p) d -> p t d", p=P)).then_inc(s.x_in, 16)
            pool.dma_start(gp[:], t["g_post"].partition_broadcast(P)).then_inc(s.bcast_in, 16)
            pool.dma_start(bgate[:], t["b_ada"][:, 2 * D:3 * D].partition_broadcast(P)).then_inc(s.bcast_in, 16)
            for n, name in enumerate(("lambda_q1_2", "lambda_k1_2", "lambda_q2_2", "lambda_k2_2")):
                pool.dma_start(lam4[:, n, :], t[name].partition_broadcast(P)).then_inc(s.bcast_in, 16)
            pool.dma_start(sinks[:], t["sinks"].partition_broadcast(P)).then_inc(s.bcast_in, 16)
            pool.dma_start(fbias[:], t["b_fgate"].rearrange("a h -> h a")).then_inc(s.bcast_in, 16)
            pool.dma_start(pos[:], t["positions"].partition_broadcast(P)).then_inc(s.bcast_in, 16)
            pool.wait_ge(s.xn_done, 4)
            pool.dma_start(rot[:], t["consts"][:, K_ROT:K_ROT + P]).then_inc(s.rot_in, 16)
            pool.wait_ge(s.kvm_ready, 8)
            banks.wait_empty(pool, ("mv", 3, 0))
            pool.dma_start(mem_scratch, kvm[:]).then_inc(s.kvm_out, 16)
            pool.wait_ge(s.o_lo, 8)
            pool.dma_start(x[:], t["x"][0].rearrange("(t p) d -> p t d", p=P)).then_inc(s.x_again, 16)
            pool.wait_ge(s.x1_done, 4)
            pool.dma_start(x1_scratch, x[:]).then_inc(s.x1_out, 16)
            pool.wait_ge(s.v_lo, 13)
            pool.wait_ge(s.kvm_out, 16)
            pool.dma_start(kvm[:], mem_scratch).then_inc(s.kvm_in, 16)
            pool.wait_ge(s.v_lo, 17)
            pool.wait_ge(s.memk_lo, 4)
            pool.wait_ge(s.x1_out, 16)
            pool.dma_start(x1r[:], x1_scratch).then_inc(s.x1_in, 16)
            o_view = out[0].rearrange("(t p) d -> p t d", p=P)
            for g in range(4):
                for pair in range(2):
                    banks.wait_empty(pool, ("w2", g, pair))
                    pool.dma_start(o_view[:, 2 * pair:2 * pair + 2, 256 * g:256 * g + 256],
                                   x1r[:, 2 * pair:2 * pair + 2, 256 * g:256 * g + 256]).then_inc(s.out_sem, 16)
            pool.wait_ge(s.out_sem, 16 * 8)

        def v8(name):
            return vec[:, VEC[name][0]:VEC[name][0] + VEC[name][1]]

        def pt_key(n):
            return ("PT", n) if n < 64 else ("DT", n - 64) if n < 96 else ("XT", n - 96)

        @block.scalar
        def _(act):
            split = [0]
            rms = [0]
            th_free = [None]

            def ahead(name):
                while split[0] < len(CHUNKS):
                    nxt = CHUNKS[split[0]]
                    prev = BEFORE[nxt]
                    if prev is not None:
                        if name is None or NCH[prev] > NCH[name]:
                            return
                        banks.wait_full(act, done_by[prev])
                    wait_raw(act, nxt)
                    act.activation(wh[:, SLOT[nxt]], raw[:, NRAW[nxt] % RAWS], ACT.Copy).then_inc(s.w_hi, 1)
                    split[0] += 1

            def root(ap):
                rms[0] += 1
                act.wait_ge(s.ms_done, rms[0])
                act.activation(ap, ap, ACT.Sqrt).then_inc(s.rms_done, 1)

            def tanh_of(key):
                if th_free[0] is not None:
                    banks.wait_empty(act, th_free[0])
                banks.wait_full(act, key)
                return act.activation(th[:], ps[banks.where[key][0]][:], ACT.Tanh, scale=0.5)

            def gate_of(key):
                tanh_of(key).then_inc(s.tanhed, 1)
                th_free[0] = key
                ahead(key)

            junk = qf[:].rearrange("p a n -> p (a n)")
            squares = [0]

            def square_rows(src, dst, tiles):
                for tt in range(tiles):
                    if squares[0]:
                        act.wait_ge(s.sumsq, squares[0])
                    act.activation(junk, src[:, tt, :], ACT.Square, accum_out=dst[:, tt:tt + 1]).then_inc(s.sumsq, 1)
                    squares[0] += 1

            act.wait_ge(s.mem_in, 16)
            square_rows(memx, MEM_SS, 2)
            banks.wait_full(act, "vec")
            ins = act.activation(vec[:], ps[7][:, 0:NVEC], ACT.Copy)
            banks.empty(ins, "vec")
            root(MEM_SS)
            act.wait_ge(s.vec_done, 1)
            act.activation(tc_, v8("c"), ACT.Tanh, scale=0.5).then_inc(s.c_tanh, 1)
            act.wait_ge(s.lam_done, 1)
            act.activation(lsum, lsum, ACT.Exp).then_inc(s.lam_done, 1)
            ahead(None)
            for g in range(4):
                banks.wait_full(act, ("memT", g))
                for i in range(2):
                    c = 2 * g + i
                    act.activation(hh[:, c, 0:MEM], ps[2 + g % 2][:, MEM * i:MEM * i + MEM], ACT.Identity,
                                   scale=v("mem_g", c)).then_inc(s.h_hi, 1)
            act.wait_ge(s.x_in, 16)
            square_rows(x, X_SS, T)
            root(X_SS)
            for h in range(4):
                key = ("mk", h, "k")
                b = banks.where[key][0]
                banks.wait_full(act, key)
                if h > 0:
                    banks.wait_full(act, ("mks", h - 1))
                act.activation(sq[:], ps[b][:], ACT.Square).then_inc(s.squared, 1)
                banks.empty(act.activation(km[:, 2 * h:2 * h + 2, :], ps[b][:].rearrange("p (c n) -> p c n", n=MEM),
                                           ACT.Copy), key)
                ahead(("mk", 2 * h + 1))
            for g in range(4):
                key = ("mv", g, 0)
                b = banks.where[key][0]
                banks.wait_full(act, key)
                banks.empty(act.activation(vm[:, :, MEM * g:MEM * g + MEM], ps[b][:].rearrange("p (c n) -> p c n", n=MEM),
                                           ACT.Copy), key)
                ahead(("mv", 2 * g + 1))
            root(rsm[:])
            act.wait_ge(s.mod_done, 1)
            for c in range(C):
                key = ("xT", c)
                tmp = (mx, gj)[c % 2]
                banks.wait_full(act, key)
                if c >= 2:
                    act.wait_ge(s.h_lo, c - 1)
                banks.empty(act.activation(tmp[:], ps[2 + c % 2][:], ACT.Identity, scale=scale_a[:, c:c + 1],
                                           bias=modc[:, c:c + 1]), key)
                banks.wait_empty(act, key)
                act.activation(hh[:, c, :], tmp[:], ACT.Copy).then_inc(s.h_hi, 1)
            act.wait_ge(s.cum_dve, 1)
            f, e, l, cum = (cumt[0:8, n, :] for n in range(4))
            act.activation(e, f, ACT.Abs).then_inc(s.cum_act, 1)
            act.wait_ge(s.cum_act, 1)
            act.activation(e, e, ACT.Exp, scale=-1.0).then_inc(s.cum_act, 1)
            act.wait_ge(s.cum_act, 2)
            act.activation(e, e, ACT.Ln, bias=ones[0:8, 0:1]).then_inc(s.cum_act, 1)
            ahead(("fa", 0))

            def raw_q(key, i, free):
                banks.wait_full(act, key)
                act.wait_ge(s.q_lo, free)
                banks.empty(act.activation(qf[:, i, :], ps[banks.where[key][0]][:], ACT.Copy), key)
                ahead(key)

            raw_q(("qa", 0), 0, 0)
            act.wait_ge(s.kvm_out, 16)
            for g in range(2):
                for pair in range(2):
                    key = ("va", g, pair)
                    banks.wait_full(act, key)
                    banks.empty(act.activation(va[:, 2 * pair:2 * pair + 2, 256 * g:256 * g + 256],
                                               ps[banks.where[key][0]][:].rearrange("p (t n) -> p t n", n=256),
                                               ACT.Copy), key)
                ahead(("va", 2 * g + 1))
            raw_q(("ka", 0), 1, 0)
            act.wait_ge(s.cum_dve, 2)
            act.activation(negcum[0:8, 0, :], cum, ACT.Copy, scale=-1.0).then_inc(s.cum_hi, 1)

            def split_q(i, src, last_scores, scale=1.0):
                if last_scores is not None:
                    banks.wait_full(act, last_scores)
                act.activation((qh, kh)[i], src, ACT.Copy, scale=scale).then_inc(s.q_hi, 1)

            def exp_unit(u_, key, w, sink=None):
                act.wait_ge(s.negmax, u_ + 1)
                if u_ >= 2:
                    banks.wait_full(act, pt_key(u_ - 2))
                b = banks.where[key][0]
                col = u_ % 16
                lo = 256 - w if sink is not None else 0
                banks.empty(act.activation(prob[:, u_ % 2, lo:lo + w], ps[b][:, lo:lo + w], ACT.Exp,
                                           bias=stat[:, 0, col:col + 1], accum_out=stat[:, 1, col:col + 1]), key)
                if sink is not None:
                    act.activation(esink[:, col:col + 1], sinks[:, sink:sink + 1], ACT.Exp,
                                   bias=stat[:, 0, col:col + 1]).then_inc(s.expd, 1)

            def pt_hi(u_, dst, last_values, view=None):
                key = pt_key(u_)
                banks.wait_full(act, key)
                if last_values is not None:
                    banks.wait_full(act, last_values)
                act.activation(dst, view, ACT.Copy).then_inc(s.pt_hi, 1)

            def split_v(src, last_values):
                if last_values is not None:
                    banks.wait_full(act, last_values)
                act.activation(vh, src, ACT.Copy).then_inc(s.v_hi, 1)

            def split_o(c, scale=0.5, last=None, mixed=None, parts=()):
                if last is not None:
                    banks.wait_full(act, last)
                if mixed is not None:
                    act.wait_ge(s.mixed, mixed)
                for key in parts:
                    banks.wait_empty(act, key)
                act.activation(oh[:, c, :], mx[:], ACT.Copy, scale=scale).then_inc(s.o_hi, 1)

            for c in range(4):
                fill = [("qa", c + 1), ("ka", c + 1), ("za", c), ("zb", c)] if c < 3 else \
                    [("kb", 0), ("vb", 0), ("za", 3), ("zb", 3)]
                banks.wait_empty(act, ("qa", c))
                banks.wait_empty(act, ("ka", c))
                for i in range(2):
                    split_q(i, qf[:, i, :], ("S", 8 * c - 1) if c else None, (0.125, 1.0)[i])
                for k in range(8 + 3):
                    if k < 8:
                        exp_unit(8 * c + k, ("S", 8 * c + k), P * (k % 4 + 1))
                    if k % 2 == 1 and k < 8:
                        key = fill[k // 2]
                        if key[0] in ("qa", "ka", "kb"):
                            raw_q(key, 1 if key[0] == "ka" else 0, 2 * c + 2)
                        elif key[0] == "vb":
                            banks.wait_full(act, key)
                            banks.empty(act.activation(vb[:].rearrange("p t n -> p (t n)"),
                                                       ps[banks.where[key][0]][:], ACT.Copy), key)
                            ahead(key)
                        else:
                            gate_of(key)
                    if 0 <= k - 2 < 8:
                        u_ = 8 * c + k - 2
                        n = u_ % 4
                        pt_hi(u_, pth[:, 0:n + 1, n * P:n * P + P], ("PO", u_ // 4 - 1) if u_ >= 4 else None,
                              ps[6][:, 0:n * P + P].rearrange("p (b n) -> p b n", n=P))
                    if k == 3:
                        if c == 0:
                            banks.wait_empty(act, ("va", 1, 1))
                        split_v(va[:, :, c * P:c * P + P], ("PO", 2 * c - 1) if c else None)
                    if k == 10:
                        split_o(c, parts=[("PO", 2 * c), ("PO", 2 * c + 1)])
                if c == 0:
                    for i, dst in enumerate((sin, cos)):
                        act.wait_ge(s.rope_in, i + 1)
                        act.activation(dst[:], gzb[:, 2, :], ACT.Sin).then_inc(s.rope_out, 1)

            act.wait_ge(s.roped, 1)
            split_q(1, qf[:, 1, :], ("S", 31))
            banks.wait_full(act, ("rot", "kb", 0))
            raw_q(("qb", 0), 0, 8)
            act.wait_ge(s.roped, 2)
            split_q(0, qf[:, 1, :], ("S", 31), 0.125)
            banks.wait_empty(act, ("vb", 0))
            split_v(vb[:], ("PO", 7))
            for i in range(4):
                for k in range(8 + 3):
                    n = 8 * i + k
                    if k < 8:
                        exp_unit(32 + n, ("S", 32 + n), P if k % 4 == 0 else 2 * P, sink=i + 4 * (k // 4))
                    if k == 3 and i < 3:
                        banks.wait_full(act, ("rot", "qb", i))
                        raw_q(("qb", i + 1), 0, 10 + i)
                    if 0 <= k - 2 < 8:
                        m = n - 2
                        tt = m % 4
                        kb = max(tt - 1, 0)
                        pt_hi(32 + m, pth[:, kb:tt + 1, tt * P:tt * P + P], ("PO", 8 + m // 4 - 1),
                              ps[6][:, 0:(tt + 1 - kb) * P].rearrange("p (b n) -> p b n", n=P))
                    if k == 10:
                        split_o(4 + i, parts=[("PO", 8 + 2 * i), ("PO", 9 + 2 * i)])
                if i < 3:
                    act.wait_ge(s.roped, i + 3)
                    split_q(0, qf[:, 1, :], ("S", 32 + 8 * i + 7), 0.125)

            act.wait_ge(s.v_lo, 5)
            for g in range(4):
                for pair in range(2):
                    key = ("wo", g, pair)
                    banks.wait_full(act, key)
                    banks.empty(act.activation(ytok[:, 2 * pair:2 * pair + 2, 256 * g:256 * g + 256],
                                               ps[banks.where[key][0]][:].rearrange("p (t n) -> p t n", n=256),
                                               ACT.Copy), key)
                ahead(("wo", 2 * g + 1))
            act.wait_ge(s.q_lo, 13)
            for g in range(4):
                for pair in range(2):
                    banks.wait_empty(act, ("wo", g, pair))
            square_rows(ytok, Y_SS, T)
            root(Y_SS)
            for tt in range(T):
                act.wait_ge(s.x1_done, tt + 1)
                square_rows(x[:, tt:tt + 1, :], X1_SS[:, tt:tt + 1], 1)
            root(X1_SS)
            for c in range(C):
                key = ("x1T", c)
                banks.wait_full(act, key)
                act.activation(hh[:, c, :], ps[2 + c % 2][:], ACT.Identity, scale=v("norm_g", c)).then_inc(s.h_hi, 1)
            for g in range(4):
                for pair in range(2):
                    key = ("dv", g, pair)
                    banks.wait_full(act, key)
                    banks.empty(act.activation(dv[:, 2 * pair:2 * pair + 2, 256 * g:256 * g + 256],
                                               ps[banks.where[key][0]][:].rearrange("p (t n) -> p t n", n=256),
                                               ACT.Copy), key)
                ahead(("dv", 2 * g + 1))
            raw_q(("dq", 0), 0, 13)
            raw_q(("dk", 0), 1, 13)

            def square_q(i, key, last_total):
                banks.wait_empty(act, key)
                banks.wait_full(act, last_total)
                act.activation(sq[:], qf[:, i, :], ACT.Square).then_inc(s.squared, 1)

            square_q(0, ("dq", 0), ("mks", 3))
            root(rs[:])
            square_q(1, ("dk", 0), ("dns", 0))
            root(rs[:])

            def of_copy(j):
                banks.wait_full(act, ("DO", j))
                banks.wait_full(act, ("dns", min(2 * j + 3, 15)))
                act.wait_ge(s.o_lo, 8 + j)
                act.activation(sq[:], ps[7][:], ACT.Square).then_inc(s.of_copied, 1)
                banks.empty(act.activation(mx[:], ps[7][:], ACT.Copy), ("DO", j))

            def diff_pt_hi(u_):
                n = u_ % 4
                pt_hi(64 + u_, pth[:, 0:n + 1, n * P:n * P + P],
                      ("DO", u_ // 4 - 1) if u_ >= 4 else ("PO", 15),
                      ps[6][:, 0:n * P + P].rearrange("p (b n) -> p b n", n=P))

            for j in range(8):
                act.wait_ge(s.qn_done, 2 * j + 2)
                for i in range(2):
                    split_q(i, qf[:, i, :], ("D", 4 * j - 1, 1) if j else ("S", 63))
                for tt in range(4):
                    u_ = 4 * j + tt
                    w = P * (tt + 1)
                    if tt < 2 and j < 7:
                        raw_q((("dq", "dk")[tt], j + 1), tt, 13 + 2 * j + 2)
                    if tt == 2:
                        banks.empty(tanh_of(("gb", j)), ("gb", j))
                        th_free[0] = ("ga", j)
                        ahead(("gb", j))
                        banks.wait_full(act, ("ga", j))
                        ahead(("ga", j))
                        if j > 0:
                            split_o(j - 1, last=("wo", 3, 1), mixed=j)
                    if tt == 3:
                        gate_of(("dg", j))
                        if j < 7:
                            root(rs[:])
                    for m in range(2):
                        key = ("D", u_, m)
                        col = (2 * u_ + m) % 16
                        act.wait_ge(s.negmax, 64 + 2 * u_ + m + 1)
                        if m == 0:
                            banks.wait_full(act, pt_key(64 + u_ - 2))
                        elif u_ > 0:
                            act.wait_ge(s.prob_ready, 64 + u_)
                        banks.empty(act.activation(prob[:, u_ % 2 if m == 0 else 2, 0:w], ps[banks.where[key][0]][:, 0:w],
                                                   ACT.Exp, bias=stat[:, 0, col:col + 1],
                                                   accum_out=stat[:, 1, col:col + 1]), key)
                    if u_ > 0:
                        diff_pt_hi(u_ - 1)
                    if tt == 0 and j > 0:
                        of_copy(j - 1)
                    if tt == 1:
                        if j > 0:
                            root(rs[:])
                        split_v(dv[:, :, j * P:j * P + P], ("DO", j - 1) if j else ("PO", 15))
                    if tt in (2, 3) and j < 7:
                        i = tt - 2
                        square_q(i, (("dq", "dk")[i], j + 1),
                                 ("dns", 2 * j + 2) if i else (("sub", j - 1) if j else ("dns", 1)))
                if j < 7:
                    root(rs[:])
            diff_pt_hi(31)
            of_copy(7)

            def branch(b, tail=None):
                for j in range(8):
                    banks.empty(tanh_of(("m" + b, j)), ("m" + b, j))
                    th_free[0] = ("p" + b, j)
                    ahead(("m" + b, j))
                    if j == 0 and tail:
                        tail()
                    banks.wait_full(act, ("p" + b, j))
                    ahead(("p" + b, j))

            def diff_tail():
                root(rs[:])
                split_o(7, mixed=8)

            branch("d", diff_tail)

            def x_squares(h):
                for i in range(2):
                    banks.wait_empty(act, ("xq", 2 * h + i))
                banks.wait_full(act, ("sub", 7) if h == 0 else ("xns", h - 1))
                act.wait_ge(s.qn_done, 16 + 2 * h)
                if h == 0:
                    act.wait_ge(s.mixed, 8)
                act.activation(sq[:], qf[:, 0, :], ACT.Square)
                act.activation(rs[:], qf[:, 1, :], ACT.Square).then_inc(s.squared, 1)

            for i in range(2):
                raw_q(("xq", i), i, 29)
            x_squares(0)
            root(rs[:])
            act.wait_ge(s.kvm_in, 16)
            act.wait_ge(s.conv_done, 8)

            def x_pt_hi(u_):
                pr = u_ % 2
                pt_hi(96 + u_, pth[:, 0:2, 256 * pr:256 * pr + 256], ("XO", u_ // 2 - 1, 1) if u_ >= 2 else ("DO", 7),
                      ps[6][:].rearrange("p (b n) -> p b n", n=256))

            def x_split_o(h):
                for i in range(2):
                    split_o(2 * h + i, last=("pd", 7), parts=[("XO", h, i)])

            for h in range(4):
                act.wait_ge(s.qn_done, 16 + 2 * h + 2)
                last = ("X", 2 * h - 1) if h else ("D", 31, 1)
                for i in range(2):
                    split_q(i, qf[:, i, :], last)
                act.activation(xk[:, 0], km[:, 2 * h:2 * h + 2, :], ACT.Copy).then_inc(s.memk_hi, 1)
                for pr in range(2):
                    u_ = 2 * h + pr
                    for i in range(2):
                        if pr == 0 and h < 3:
                            raw_q(("xq", 2 * h + 2 + i), i, 29 + 2 * h + 2)
                        if pr == 1:
                            gate_of(("xg", 2 * h + i))
                    key = ("X", u_)
                    act.wait_ge(s.negmax, 128 + u_ + 1)
                    banks.wait_full(act, pt_key(96 + u_ - 2))
                    for tt in range(2):
                        col = (2 * u_ + tt) % 16
                        ins = act.activation(prob[:, u_ % 2, 256 * tt:256 * tt + 256],
                                             ps[banks.where[key][0]][:, 256 * tt:256 * tt + 256], ACT.Exp,
                                             bias=stat[:, 0, col:col + 1], accum_out=stat[:, 1, col:col + 1])
                    banks.empty(ins, key)
                    if u_ > 0:
                        x_pt_hi(u_ - 1)
                    if pr == 0:
                        if h > 0:
                            x_split_o(h - 1)
                        split_v(vm[:, :, MEM * h:MEM * h + MEM].rearrange("p k (i n) -> p k i n", n=P),
                                ("XO", h - 1, 1) if h else ("DO", 7))
                    if pr == 1 and h < 3:
                        x_squares(h + 1)
                if h < 3:
                    root(rs[:])
            x_pt_hi(7)
            x_split_o(3)
            branch("x")

            for j in range(C):
                act.wait_ge(s.ln_centred, j + 1)
                if j >= 2:
                    act.wait_ge(s.lnx, j - 1)
                elif j == 0:
                    act.wait_ge(s.o_lo, 24)
                    banks.wait_full(act, "ln_sum")
                act.activation((sq, mx)[j % 2][:], u[:, j, PAD:], ACT.Square).then_inc(s.ln_act, 1)
            root(rs[:])
            for j in range(C):
                gate_of(("cg", j))
                act.wait_ge(s.ln_scaled, j + 1)
                if j > 0:
                    act.wait_ge(s.mixed, 8 + j)
                act.activation(qf[:, 0, :], u[:, j, PAD:], ACT.Identity, scale=v("ln_g", j), bias=v("ln_b", j))\
                   .then_inc(s.ln_t, 1)
                act.wait_ge(s.ln_t, 2 * j + 1)
                act.activation(qf[:, 1, :], qf[:, 0, :], ACT.Tanh, scale=0.5).then_inc(s.ln_t, 1)
                split_o(j, 0.25, ("px", 7), mixed=8 + j + 1)
            def y_hi(j):
                act.wait_ge(s.y_sum, 8 + j + 1)
                act.activation(hh[:, j, :], y[:, j, :], ACT.Copy, scale=0.5).then_inc(s.yhi, 1)

            for j in range(8):
                banks.empty(tanh_of(("mc", j)), ("mc", j))
                th_free[0] = ("pc", j)
                ahead(("mc", j))
                if j == 7:
                    for i in range(6):
                        y_hi(i)
                banks.wait_full(act, ("pc", j))
                ahead(("pc", j))
            y_hi(6)
            y_hi(7)
            for g in range(4):
                for pair in range(2):
                    banks.wait_full(act, ("w2", g, pair))
                ahead(("w2", 2 * g + 1))

        @block.vector
        def _(dve):
            split = [0]
            rms = [0]
            steps = [0]
            gates = [0]

            def then(ins):
                steps[0] += 1
                ins.then_inc(s.dve_step, 1)
                dve.wait_ge(s.dve_step, steps[0])

            def bank(key):
                return ps[banks.where[key][0]]

            def ada_group(g):
                slot = NRAW[("ada", 2 * g)] % RAWS
                wait_raw(dve, ("ada", 2 * g))
                wait_raw(dve, ("ada", 2 * g + 1))
                for c in range(C):
                    dst = (acc_even, acc_odd)[c % 2][:, 256 * g:256 * g + 256].rearrange("p (a n) -> p a n", a=2)
                    if c >= 2:
                        dve.wait_ge(s.ada_step, 6 * g + c - 1)
                        ins = dve.scalar_tensor_tensor(dst, raw[:, slot:slot + 2, c, :], cc_[:, c:c + 1], dst,
                                                       ALU.mult, ALU.add)
                    else:
                        ins = dve.tensor_scalar(dst, raw[:, slot:slot + 2, c, :], cc_[:, c:c + 1], None, ALU.mult)
                    if c < C - 2:
                        ins.then_inc(s.ada_step, 1)
                ins.then_inc(s.raw_used, 2)

            def ahead(name):
                while split[0] < len(CHUNKS):
                    n = split[0]
                    nxt = CHUNKS[n]
                    prev = BEFORE[nxt]
                    if prev is not None and (name is None or NCH[prev] > NCH[name]):
                        return
                    if n in (4, 6, 8, 10, 12, 14):
                        ada_group(n - 4)
                        ada_group(n - 3)
                    dve.wait_ge(s.w_hi, n + 1)
                    w = SLOT[nxt]
                    dve.tensor_tensor(wl[:, w], raw[:, NRAW[nxt] % RAWS], wh[:, w].bitcast(F32), ALU.subtract)\
                       .then_inc(s.raw_used, 1)
                    split[0] += 1

            def mean_square(dst, src, n, eps, key=None, root_=True):
                ins = dve.tensor_scalar(dst, src, 1.0 / n, eps, ALU.mult, ALU.add)
                if key is not None:
                    banks.empty(ins, key)
                    banks.wait_empty(dve, key)
                else:
                    then(ins)
                if root_:
                    dve.reciprocal(dst, dst).then_inc(s.ms_done, 1)
                    rms[0] += 1

            def wait_root():
                dve.wait_ge(s.rms_done, rms[0])

            dve.wait_ge(s.const_in, 16 * 4)
            dve.tensor_copy(masks[:].rearrange("p a n -> p (a n)"), kload[:, 0:2 * P])
            dve.tensor_copy(ident_b[:], ident[:])
            dve.tensor_copy(dist[:], kload[:, K_DIST - K_PREV:K_DIST - K_PREV + S])
            dve.tensor_copy(freq, kload[:, K_FREQ - K_PREV:K_FREQ - K_PREV + 1])
            for j in range(8):
                ins = dve.tensor_scalar(slopes[:, j, :], ident[:], 2.0 ** -(j + 1), None, ALU.mult)
            then(ins)
            dve.wait_ge(s.sumsq, 2)
            mean_square(MEM_SS, MEM_SS, D, 1e-6)
            wait_root()
            for tt in range(2):
                dve.tensor_scalar(memx[:, tt, :], memx[:, tt, :], MEM_SS[:, tt:tt + 1], None, ALU.mult).then_inc(s.nk_done, 1)
            banks.wait_full(dve, "taps")
            banks.empty(dve.tensor_scalar(taps[:], ps[6][:, 0:TAPS * C], 0.5, None, ALU.mult), "taps")
            banks.wait_empty(dve, "vec")
            dve.tensor_scalar(v("dqn"), v("dqn"), HD ** -0.5, None, ALU.mult)
            dve.tensor_scalar(v8("xqn"), v8("xqn"), 256 ** -0.5, None, ALU.mult)
            dve.tensor_scalar(v("subln"), v("subln"), 1.0 - LAMBDA_INIT, None, ALU.mult).then_inc(s.vec_done, 1)
            dve.wait_ge(s.bcast_in, 16 * 9)
            for i in range(2):
                ins = dve.tensor_tensor_reduce(gj[:, HD * i:HD * i + HD], lam4[:, 2 * i, :], lam4[:, 2 * i + 1, :], 1.0, 0.0, ALU.mult,
                                               ALU.add, lsum[:, i:i + 1])
            ins.then_inc(s.lam_done, 1)
            dve.wait_ge(s.c_tanh, 1)
            then(dve.scalar_tensor_tensor(cc_, tc_, 1.0, v8("c"), ALU.add, ALU.mult))
            then(dve.tensor_scalar(cc_, cc_, 0.5, None, ALU.mult))
            dve.wait_ge(s.lam_done, 2)
            then(dve.tensor_tensor(nlam, lsum[:, 1:2], lsum[:, 0:1], ALU.subtract))
            dve.tensor_scalar(nlam, nlam, -LAMBDA_INIT, None, ALU.add)
            dve.tensor_scalar(nsinks, sinks, -1.0, None, ALU.mult).then_inc(s.const_done, 1)
            dve.wait_ge(s.const_done, 1)
            ahead(None)
            for g in range(4):
                dve.wait_ge(s.h_hi, 2 * g + 2)
                for i in range(2):
                    c = 2 * g + i
                    ins = dve.scalar_tensor_tensor(hl[:, c, 0:MEM], ps[2 + g % 2][:, MEM * i:MEM * i + MEM],
                                                   v("mem_g", c), hh[:, c, 0:MEM].bitcast(F32), ALU.mult, ALU.subtract)
                banks.empty(ins, ("memT", g))
            dve.wait_ge(s.sumsq, 6)
            mean_square(X_SS, X_SS, D, 1e-6)
            wait_root()
            for tt in range(T):
                dve.tensor_scalar(xn[:, tt, :], x[:, tt, :], X_SS[:, tt:tt + 1], None, ALU.mult).then_inc(s.xn_done, 1)

            def mem_sums(h):
                key = ("mks", h)
                banks.wait_full(dve, key)
                banks.empty(dve.tensor_scalar(rsm[:, MEM * h:MEM * h + MEM], ps[7][:, 0:MEM], 1.0 / MEM, 1e-6,
                                              ALU.mult, ALU.add), key)

            for h in range(4):
                banks.wait_full(dve, ("mk", h, "k"))
                if h > 0:
                    mem_sums(h - 1)
                ahead(("mk", 2 * h + 1))
            for g in range(4):
                if g == 1:
                    mem_sums(3)
                    banks.wait_empty(dve, ("mks", 3))
                    dve.reciprocal(rsm[:], rsm[:]).then_inc(s.ms_done, 1)
                    rms[0] += 1
                banks.wait_full(dve, ("mv", g, 0))
                ahead(("mv", 2 * g + 1))
            wait_root()
            for c in range(C):
                banks.wait_empty(dve, ("mk", c // 2, "k"))
                dve.scalar_tensor_tensor(km[:, c, :], km[:, c, :], v("xkn", c % 2),
                                         rsm[:, MEM * (c // 2):MEM * (c // 2) + MEM], ALU.mult, ALU.mult)\
                   .then_inc(s.kvm_ready, 1)
            banks.wait_full(dve, "mod")
            banks.empty(dve.tensor_tensor(modc, ps[7][:, 0:16], v8("b_ada"), ALU.add), "mod")
            banks.wait_empty(dve, "mod")
            dve.scalar_tensor_tensor(scale_a, modc[:, 8:16], 1.0, v8("g_pre"), ALU.add, ALU.mult).then_inc(s.mod_done, 1)
            for k in range(2):
                banks.wait_full(dve, ("gate", k))
            for k in range(2):
                cols = slice(S * k, S * k + S)
                banks.empty(dve.tensor_tensor(gate[:, cols], ps[4 + k][:], bgate[:, cols], ALU.add), ("gate", k))
            for k in range(2):
                banks.wait_empty(dve, ("gate", k))
            then(dve.tensor_tensor(gate[:], gate[:], gp[:], ALU.mult))
            for h in range(8):
                dve.tensor_copy(sel[0:8, h, :], ident[0:8, h:h + 1].to_broadcast([8, P]))
            for c in range(C):
                dve.wait_ge(s.h_hi, 8 + c + 1)
                dve.tensor_tensor(hl[:, c, :], (mx, gj)[c % 2][:], hh[:, c, :].bitcast(F32), ALU.subtract)\
                   .then_inc(s.h_lo, 1)
            f, e, l, cum = (cumt[0:8, n, :] for n in range(4))
            key = ("fa", 0)
            banks.wait_full(dve, key)
            banks.empty(dve.tensor_scalar(f, bank(key)[0:8, :], fbias, None, ALU.add), key)
            banks.wait_empty(dve, key)
            dve.memset(l, 1.0).then_inc(s.cum_dve, 1)
            ahead(key)
            dve.wait_ge(s.cum_act, 3)
            then(dve.scalar_tensor_tensor(e, f, 0.0, e, ALU.min, ALU.subtract))
            dve.tensor_tensor_scan(cum, l, e, 0.0, ALU.mult, ALU.add).then_inc(s.cum_dve, 1)
            banks.wait_full(dve, ("qa", 0))
            ahead(("qa", 0))
            for g in range(2):
                banks.wait_full(dve, ("va", g, 1))
                ahead(("va", 2 * g + 1))
            dve.wait_ge(s.cum_hi, 1)
            dve.scalar_tensor_tensor(negcum[0:8, 1, :], cum, -1.0, negcum[0:8, 0, :].bitcast(F32), ALU.mult, ALU.subtract)\
               .then_inc(s.cum_done, 1)
            banks.wait_full(dve, ("ka", 0))
            ahead(("ka", 0))

            def split_q(i, n, src, scale=1.0):
                dve.wait_ge(s.q_hi, n)
                dve.scalar_tensor_tensor((ql, kl)[i], src, scale, (qh, kh)[i].bitcast(F32), ALU.mult, ALU.subtract)\
                   .then_inc(s.q_lo, 1)

            def split_v(n, src):
                dve.wait_ge(s.v_hi, n)
                dve.tensor_tensor(vl, src, vh.bitcast(F32), ALU.subtract).then_inc(s.v_lo, 1)

            def split_o(c, n, scale=0.5):
                dve.wait_ge(s.o_hi, n)
                dve.scalar_tensor_tensor(ol[:, c, :], mx[:], scale, oh[:, c, :].bitcast(F32), ALU.mult, ALU.subtract)\
                   .then_inc(s.o_lo, 1)

            def gate_to(key, dst):
                gates[0] += 1
                dve.wait_ge(s.tanhed, gates[0])
                banks.wait_full(dve, key)
                banks.empty(dve.scalar_tensor_tensor(dst, th[:], 1.0, bank(key)[:], ALU.add, ALU.mult), key)
                banks.wait_empty(dve, key)
                ahead(key)

            def normalise(u_, key, w, sink=False):
                col = u_ % 16
                lo = 256 - w if sink else 0
                r = stat[:, 2, col:col + 1]
                banks.wait_empty(dve, key)
                if sink:
                    dve.wait_ge(s.expd, u_ - 31)
                    then(dve.tensor_tensor(stat[:, 1, col:col + 1], stat[:, 1, col:col + 1], esink[:, col:col + 1], ALU.add))
                then(dve.reciprocal(r, stat[:, 1, col:col + 1]))
                dve.tensor_scalar(prob[:, u_ % 2, lo:lo + w], prob[:, u_ % 2, lo:lo + w], r, None, ALU.mult)\
                   .then_inc(s.prob_ready, 1)

            def pt_lo(u_, dst, hi, view):
                dve.wait_ge(s.pt_hi, u_ + 1)
                banks.empty(dve.tensor_tensor(dst, view, hi.bitcast(F32), ALU.subtract), pt_key(u_))

            for c in range(4):
                fill = [("qa", c + 1), ("ka", c + 1), ("za", c), ("zb", c)] if c < 3 else \
                    [("kb", 0), ("vb", 0), ("za", 3), ("zb", 3)]
                for i in range(2):
                    split_q(i, 2 * c + i + 1, qf[:, i, :], (0.125, 1.0)[i])
                for k in range(8 + 3):
                    u_ = 8 * c + k
                    if k < 8:
                        w = P * (k % 4 + 1)
                        banks.wait_full(dve, ("S", u_))
                        dve.reduce_max(stat[:, 0, u_ % 16:u_ % 16 + 1], bank(("S", u_))[:, 0:w], AX, negate=True)\
                           .then_inc(s.negmax, 1)
                    if k % 2 == 1 and k < 8:
                        key = fill[k // 2]
                        if key[0] == "za":
                            gate_to(key, gj[:])
                        elif key[0] == "zb":
                            gate_to(key, gzb[:, c, :])
                        else:
                            banks.wait_full(dve, key)
                            ahead(key)
                    if 1 <= k < 9:
                        normalise(u_ - 1, ("S", u_ - 1), P * ((k - 1) % 4 + 1))
                    if 0 <= k - 2 < 8:
                        n = (k - 2) % 4
                        pt_lo(u_ - 2, ptl[:, 0:n + 1, n * P:n * P + P], pth[:, 0:n + 1, n * P:n * P + P],
                              ps[6][:, 0:n * P + P].rearrange("p (b n) -> p b n", n=P))
                    if k == 3:
                        split_v(c + 1, va[:, :, c * P:c * P + P])
                    if k >= 6 and (k - 3) % 4 == 3:
                        i = (k - 3) // 4
                        key = ("PO", 2 * c + i)
                        half = slice(HD * i, HD * i + HD)
                        banks.wait_full(dve, key)
                        banks.empty(dve.tensor_tensor(mx[half, :], ps[7][half, :], gj[half, :], ALU.mult), key)
                    if k == 10:
                        for i in range(2):
                            banks.wait_empty(dve, ("PO", 2 * c + i))
                        split_o(c, c + 1)
                if c == 0:
                    ang, turns, r = ca[:, 1, :], gzb[:, 3, :], gzb[:, 2, :]
                    then(dve.tensor_copy(ang, pos[:]))
                    then(dve.tensor_scalar(ang, ang, freq, None, ALU.mult))
                    for i, quarter in enumerate((0.0, 0.25)):
                        then(dve.tensor_scalar(turns, ang, 0.15915494309189535, quarter, ALU.mult, ALU.add))
                        then(dve.tensor_scalar(turns, turns, MAGIC, None, ALU.add))
                        then(dve.tensor_scalar(turns, turns, -MAGIC, None, ALU.add))
                        if i == 1:
                            dve.wait_ge(s.rope_out, 1)
                        then(dve.scalar_tensor_tensor(r, turns, -TWO_PI_A, ang, ALU.mult, ALU.add))
                        then(dve.scalar_tensor_tensor(r, turns, -TWO_PI_B, r, ALU.mult, ALU.add))
                        then(dve.scalar_tensor_tensor(r, turns, -TWO_PI_C, r, ALU.mult, ALU.add))
                        then(dve.tensor_scalar(r, r, quarter * 2 * np.pi, PI, ALU.add, ALU.min))
                        dve.tensor_scalar(r, r, -PI, None, ALU.max).then_inc(s.rope_in, 1)

            def rope(key, splits):
                banks.wait_empty(dve, key)
                dve.wait_ge(s.q_lo, splits)
                dve.wait_ge(s.rope_out, 2)
                then(dve.tensor_tensor(qf[:, 1, :], qf[:, 0, :], cos[:], ALU.mult))
                banks.wait_full(dve, ("rot",) + key)
                banks.empty(dve.tensor_tensor(rs[:], ps[7][:], sin[:], ALU.mult), ("rot",) + key)
                banks.wait_empty(dve, ("rot",) + key)
                dve.tensor_tensor(qf[:, 1, :], qf[:, 1, :], rs[:], ALU.add).then_inc(s.roped, 1)

            rope(("kb", 0), 8)
            split_q(1, 9, qf[:, 1, :])
            banks.wait_full(dve, ("qb", 0))
            ahead(("qb", 0))
            rope(("qb", 0), 9)
            split_q(0, 10, qf[:, 1, :], 0.125)
            split_v(5, vb[:])
            for i in range(4):
                for k in range(8 + 3):
                    n = 8 * i + k
                    u_ = 32 + n
                    if k < 8:
                        w = P if k % 4 == 0 else 2 * P
                        head = i + 4 * (k // 4)
                        m = stat[:, 0, u_ % 16:u_ % 16 + 1]
                        banks.wait_full(dve, ("S", u_))
                        then(dve.reduce_max(m, bank(("S", u_))[:, 256 - w:256], AX, negate=True))
                        dve.tensor_tensor(m, m, nsinks[:, head:head + 1], ALU.min).then_inc(s.negmax, 1)
                    if k == 3 and i < 3:
                        banks.wait_full(dve, ("qb", i + 1))
                        ahead(("qb", i + 1))
                    if 1 <= k < 9:
                        normalise(u_ - 1, ("S", u_ - 1), P if (k - 1) % 4 == 0 else 2 * P, True)
                    if 0 <= k - 2 < 8:
                        tt = (k - 2) % 4
                        kb = max(tt - 1, 0)
                        pt_lo(u_ - 2, ptl[:, kb:tt + 1, tt * P:tt * P + P], pth[:, kb:tt + 1, tt * P:tt * P + P],
                              ps[6][:, 0:(tt + 1 - kb) * P].rearrange("p (b n) -> p b n", n=P))
                    if k >= 6 and (k - 3) % 4 == 3:
                        g = (k - 3) // 4
                        key = ("PO", 8 + 2 * i + g)
                        half = slice(HD * g, HD * g + HD)
                        banks.wait_full(dve, key)
                        banks.empty(dve.tensor_tensor(mx[half, :], ps[7][half, :], gzb[half, i, :], ALU.mult), key)
                    if k == 10:
                        for g in range(2):
                            banks.wait_empty(dve, ("PO", 8 + 2 * i + g))
                        split_o(4 + i, 5 + i)
                if i < 3:
                    rope(("qb", i + 1), 10 + i)
                    split_q(0, 11 + i, qf[:, 1, :], 0.125)

            for g in range(4):
                banks.wait_full(dve, ("wo", g, 1))
                ahead(("wo", 2 * g + 1))
            dve.wait_ge(s.sumsq, 10)
            mean_square(Y_SS, Y_SS, D, 1e-6)
            wait_root()
            dve.wait_ge(s.x_again, 16)
            for tt in range(T):
                then(dve.scalar_tensor_tensor(ytok[:, tt, :], ytok[:, tt, :], Y_SS[:, tt:tt + 1], gate[:],
                                              ALU.mult, ALU.mult))
                dve.tensor_tensor(x[:, tt, :], x[:, tt, :], ytok[:, tt, :], ALU.add).then_inc(s.x1_done, 1)
            dve.wait_ge(s.sumsq, 14)
            mean_square(X1_SS, X1_SS, D, 1e-6)
            wait_root()
            for tt in range(T):
                dve.wait_ge(s.x1_done, tt + 1)
                dve.tensor_scalar(ytok[:, tt, :], x[:, tt, :], X1_SS[:, tt:tt + 1], None, ALU.mult).then_inc(s.xn_done, 1)
            for c in range(C):
                key = ("x1T", c)
                dve.wait_ge(s.h_hi, 16 + c + 1)
                banks.empty(dve.scalar_tensor_tensor(hl[:, c, :], bank(key)[:], v("norm_g", c),
                                                     hh[:, c, :].bitcast(F32), ALU.mult, ALU.subtract), key)
            for j in range(C):
                ins = dve.memset(u[:, j, 0:PAD], 0.0)
            then(ins)
            for g in range(4):
                banks.wait_full(dve, ("dv", g, 1))
                ahead(("dv", 2 * g + 1))

            normed = [0]

            def sums(key, n):
                banks.wait_full(dve, key)
                if normed[0]:
                    dve.wait_ge(s.qn_done, normed[0])
                mean_square(rs[:], ps[7][:], n, 1e-6, key)

            def norm_q(i, gain):
                wait_root()
                normed[0] += 1
                dve.scalar_tensor_tensor(qf[:, i, :], qf[:, i, :], gain, rs[:], ALU.mult, ALU.mult).then_inc(s.qn_done, 1)

            for i, name in enumerate(("dq", "dk")):
                banks.wait_full(dve, (name, 0))
                ahead((name, 0))
            for i in range(2):
                sums(("dns", i), HD)
                norm_q(i, v(("dqn", "dkn")[i]))

            taps_done = [0]
            conv_count = [0, 0]

            def conv(n, glus):
                for _ in range(n):
                    j, k = divmod(taps_done[0], TAPS)
                    if j >= glus:
                        return
                    src, w, dst = u[:, j, k:k + S], taps[:, k * C + j:k * C + j + 1], ca[:, k % 2, :]
                    if k < 2:
                        if j > 0:
                            dve.wait_ge(s.conv_done, j)
                        ins = dve.tensor_scalar(dst, src, w, v("dw_b", j) if k == 0 else None, ALU.mult,
                                                *([ALU.add] if k == 0 else []))
                    else:
                        dve.wait_ge(s.dve_step, conv_count[k % 2])
                        ins = dve.scalar_tensor_tensor(dst, src, w, dst, ALU.mult, ALU.add)
                    steps[0] += 1
                    conv_count[k % 2] = steps[0]
                    ins.then_inc(s.dve_step, 1)
                    taps_done[0] += 1
                    if k == TAPS - 1:
                        dve.wait_ge(s.dve_step, steps[0])
                        dve.tensor_tensor(u[:, j, PAD:], ca[:, 0, :], ca[:, 1, :], ALU.add).then_inc(s.conv_done, 1)

            def diff_pt_lo(u_):
                n = u_ % 4
                pt_lo(64 + u_, ptl[:, 0:n + 1, n * P:n * P + P], pth[:, 0:n + 1, n * P:n * P + P],
                      ps[6][:, 0:n * P + P].rearrange("p (b n) -> p b n", n=P))

            def diff_mix(j):
                wait_root()
                banks.wait_empty(dve, ("DO", j))
                then(dve.scalar_tensor_tensor(mx[:], mx[:], v("subln"), rs[:], ALU.mult, ALU.mult))
                dve.tensor_tensor(mx[:], mx[:], gj[:], ALU.mult).then_inc(s.mixed, 1)
                return j

            mixed_first = 16
            for j in range(8):
                for i in range(2):
                    split_q(i, 13 + 2 * j + i + 1, qf[:, i, :])
                for tt in range(4):
                    u_ = 4 * j + tt
                    w = P * (tt + 1)
                    if tt < 2 and j < 7:
                        key = (("dq", "dk")[tt], j + 1)
                        banks.wait_full(dve, key)
                        ahead(key)
                    if tt == 2:
                        if j > 0:
                            diff_mix(j - 1)
                        banks.wait_full(dve, ("gb", j))
                        ahead(("gb", j))
                        key = ("ga", j)
                        banks.wait_empty(dve, ("gb", j))
                        banks.wait_full(dve, key)
                        banks.empty(dve.scalar_tensor_tensor(u[:, j, PAD:], th[:], 1.0, bank(key)[:], ALU.add, ALU.mult), key)
                        banks.wait_empty(dve, key)
                        ahead(key)
                    if tt == 3:
                        gate_to(("dg", j), gj[:])
                    for m in range(2):
                        col = (2 * u_ + m) % 16
                        banks.wait_full(dve, ("D", u_, m))
                        dve.reduce_max(stat[:, 0, col:col + 1], bank(("D", u_, m))[:, 0:w], AX, negate=True)\
                           .then_inc(s.negmax, 1)
                    conv(6, j + 1 if tt >= 2 else j)
                    col = 2 * u_ % 16
                    r = stat[:, 2, col:col + 2]
                    for m in range(2):
                        banks.wait_empty(dve, ("D", u_, m))
                    then(dve.reciprocal(r, stat[:, 1, col:col + 2]))
                    then(dve.tensor_tensor(r[:, 1:2], r[:, 1:2], nlam, ALU.mult))
                    p0 = prob[:, u_ % 2, 0:w]
                    then(dve.tensor_scalar(p0, p0, r[:, 0:1], None, ALU.mult))
                    dve.scalar_tensor_tensor(p0, prob[:, 2, 0:w], r[:, 1:2], p0, ALU.mult, ALU.add)\
                       .then_inc(s.prob_ready, 1)
                    if u_ > 0:
                        diff_pt_lo(u_ - 1)
                    if tt == 1:
                        if j > 0:
                            sums(("sub", j - 1), P)
                        split_v(6 + j, dv[:, :, j * P:j * P + P])
                    if tt == 2 and j > 0:
                        dve.wait_ge(s.mixed, j)
                        split_o(j - 1, 8 + j)
                    if tt == 2 and j < 7:
                        sums(("dns", 2 * j + 2), HD)
                    if tt == 3 and j < 7:
                        norm_q(0, v("dqn"))
                        sums(("dns", 2 * j + 3), HD)
                        norm_q(1, v("dkn"))
            diff_pt_lo(31)

            ysum = [0]

            def branch(b, tail=None, filler=lambda: None):
                for j in range(8):
                    if j == 0:
                        banks.wait_full(dve, ("m" + b, 0))
                        ahead(("m" + b, 0))
                        if tail:
                            tail()
                    key = ("p" + b, j)
                    banks.wait_empty(dve, ("m" + b, j))
                    banks.wait_full(dve, key)
                    dst = y[:, j, :] if b == "d" else gj[:]
                    added = {"d": 0, "x": j, "c": 8 + j}[b]
                    if added:
                        dve.wait_ge(s.y_sum, added)
                    banks.empty(dve.scalar_tensor_tensor(dst, th[:], 1.0, bank(key)[:], ALU.add, ALU.mult), key)
                    banks.wait_empty(dve, key)
                    ahead(key)
                    if b != "d":
                        dve.tensor_tensor(y[:, j, :], y[:, j, :], gj[:], ALU.add).then_inc(s.y_sum, 1)
                    filler()

            def diff_tail():
                sums(("sub", 7), P)
                diff_mix(7)
                dve.wait_ge(s.mixed, 8)
                split_o(7, 16)
                dve.wait_ge(s.x1_out, 16)

            branch("d", diff_tail, lambda: conv(11, 8))

            def x_mix(h):
                for i in range(2):
                    key = ("XO", h, i)
                    banks.wait_full(dve, key)
                    dve.wait_ge(s.o_lo, 16 + 2 * h + i)
                    banks.empty(dve.tensor_tensor(mx[:], ps[7][:], (gj[:], prob[:, 2, :])[i], ALU.mult), key)
                    banks.wait_empty(dve, key)
                    split_o(2 * h + i, 16 + 2 * h + i + 1)

            for i in range(2):
                banks.wait_full(dve, ("xq", i))
                ahead(("xq", i))

            def x_norm(h):
                sums(("xns", h), 256)
                norm_q(0, v("xqn", 0))
                norm_q(1, v("xqn", 1))

            def x_pt_lo(u_):
                pr = u_ % 2
                cols = slice(256 * pr, 256 * pr + 256)
                pt_lo(96 + u_, ptl[:, 0:2, cols], pth[:, 0:2, cols], ps[6][:].rearrange("p (b n) -> p b n", n=256))

            x_norm(0)
            for h in range(4):
                for i in range(2):
                    split_q(i, 29 + 2 * h + i + 1, qf[:, i, :])
                dve.wait_ge(s.memk_hi, h + 1)
                dve.tensor_tensor(xk[:, 1], km[:, 2 * h:2 * h + 2, :], xk[:, 0].bitcast(F32), ALU.subtract)\
                   .then_inc(s.memk_lo, 1)
                for pr in range(2):
                    u_ = 2 * h + pr
                    for i in range(2):
                        if pr == 0 and h < 3:
                            key = ("xq", 2 * h + 2 + i)
                            banks.wait_full(dve, key)
                            ahead(key)
                        if pr == 1:
                            gate_to(("xg", 2 * h + i), (gj[:], prob[:, 2, :])[i])
                    key = ("X", u_)
                    col = 2 * u_ % 16
                    banks.wait_full(dve, key)
                    dve.reduce_max(stat[:, 0, col:col + 2], bank(key)[:].rearrange("p (t n) -> p t n", n=256), AX,
                                   negate=True).then_inc(s.negmax, 1)
                    banks.wait_empty(dve, key)
                    then(dve.reciprocal(stat[:, 2, col:col + 2], stat[:, 1, col:col + 2]))
                    for tt in range(2):
                        p = prob[:, u_ % 2, 256 * tt:256 * tt + 256]
                        ins = dve.tensor_scalar(p, p, stat[:, 2, col + tt:col + tt + 1], None, ALU.mult)
                    ins.then_inc(s.prob_ready, 1)
                    if u_ > 0:
                        x_pt_lo(u_ - 1)
                    if pr == 0:
                        if h > 0:
                            x_mix(h - 1)
                        split_v(14 + h, vm[:, :, MEM * h:MEM * h + MEM].rearrange("p k (i n) -> p k i n", n=P))
                    if pr == 1 and h < 3:
                        x_norm(h + 1)
            x_pt_lo(7)
            x_mix(3)
            branch("x")

            banks.wait_full(dve, "ln_sum")
            banks.empty(dve.tensor_scalar(rs[:], ps[7][:], 1.0 / D, None, ALU.mult), "ln_sum")
            banks.wait_empty(dve, "ln_sum")
            for j in range(C):
                dve.tensor_tensor(u[:, j, PAD:], u[:, j, PAD:], rs[:], ALU.subtract).then_inc(s.ln_centred, 1)
            banks.wait_full(dve, "ln_var")
            mean_square(rs[:], ps[7][:], D, 1e-5, "ln_var")
            wait_root()
            for j in range(C):
                dve.wait_ge(s.ln_centred, j + 1)
                dve.tensor_tensor(u[:, j, PAD:], u[:, j, PAD:], rs[:], ALU.mult).then_inc(s.ln_scaled, 1)
            for j in range(C):
                gate_to(("cg", j), gj[:])
                dve.wait_ge(s.ln_t, 2 * j + 2)
                then(dve.scalar_tensor_tensor(qf[:, 1, :], qf[:, 1, :], 1.0, qf[:, 0, :], ALU.add, ALU.mult))
                if j > 0:
                    dve.wait_ge(s.o_lo, 24 + j)
                dve.tensor_tensor(mx[:], qf[:, 1, :], gj[:], ALU.mult).then_inc(s.mixed, 1)
                dve.wait_ge(s.mixed, 8 + j + 1)
                split_o(j, 24 + j + 1, 0.25)

            def y_lo(j):
                dve.wait_ge(s.yhi, j + 1)
                dve.scalar_tensor_tensor(hl[:, j, :], y[:, j, :], 0.5, hh[:, j, :].bitcast(F32), ALU.mult, ALU.subtract)\
                   .then_inc(s.ylo, 1)

            branch("c")
            for j in range(8):
                y_lo(j)
            dve.wait_ge(s.x1_in, 16)
            for g in range(4):
                for pair in range(2):
                    key = ("w2", g, pair)
                    o = x1r[:, 2 * pair:2 * pair + 2, 256 * g:256 * g + 256]
                    banks.wait_full(dve, key)
                    banks.empty(dve.tensor_tensor(o, bank(key)[:].rearrange("p (t n) -> p t n", n=256), o, ALU.add), key)
                ahead(("w2", 2 * g + 1))


INPUTS = ["x", "c", "positions", "w_ada", "b_ada", "g_pre", "w_in", "b_fgate", "sinks", "w_out", "g_post", "mem_2",
          "norm_g_2", "mem_norm_g_2", "w_in_2", "conv_dw_2", "conv_dw_b_2", "conv_ln_g_2", "conv_ln_b_2",
          "w_conv_proj_2", "diff_qn_g_2", "diff_kn_g_2", "lambda_q1_2", "lambda_k1_2", "lambda_q2_2", "lambda_k2_2",
          "diff_subln_g_2", "w_diff_proj_2", "w_mem_kv_2", "x_qn_g_2", "x_kn_g_2", "w_x_proj_2", "w_out_2"]


def kernel(**inputs):
    import concourse.bacc as bacc
    from concourse.bass_utils import run_bass_kernel_spmd

    nc = bacc.Bacc("TRN2", target_bir_lowering=False, num_devices=1, dynamic_dma_scratch_size=2048)
    arrays, t = {}, {}
    for name in INPUTS:
        a = np.ascontiguousarray(inputs[name])
        arrays["in_" + name] = a
        t[name] = nc.dram_tensor("in_" + name, a.shape, mybir.dt.from_np(a.dtype), kind="ExternalInput").ap()
    arrays["in_consts"] = constants()
    t["consts"] = nc.dram_tensor("in_consts", (P, K_COLS), F32, kind="ExternalInput").ap()
    out = nc.dram_tensor("out_x", (1, S, D), F32, kind="ExternalOutput").ap()
    build(nc, t, out)
    r = run_bass_kernel_spmd(nc, [arrays], core_ids=[0])
    return r.results[0]["out_x"]
```

```python
from contextlib import ExitStack

import numpy as np

import concourse.bass as bass
from concourse import mybir

F32 = mybir.dt.float32
F32R = mybir.dt.float32r
F16 = mybir.dt.float16
BF16 = mybir.dt.bfloat16
I32 = mybir.dt.int32
ACT = mybir.ActivationFunctionType
ALU = mybir.AluOpType
AX = mybir.AxisListType.X

P = 128
D = 1024
S = 512
T = S // P
C = D // P
HD = 64
MEM = 256
TAPS = 31
PAD = TAPS - 1
MASKED = -1.0e30
MAGIC = 12582912.0
TWO_PI_A, TWO_PI_B, TWO_PI_C = 6.28125, 0.0019350051879882812, 3.0199159819e-07
PI = 3.1415925
LAMBDA_INIT = 0.8 - 0.6

K_IDENT, K_BLOCKS, K_ONES, K_ROT, K_PREV, K_CAUSAL, K_DIST, K_FREQ = 0, 128, 256, 384, 512, 640, 768, 1280
K_COLS = 1281
VEC_ROWS = [("c", 8), ("b_ada", 16), ("g_pre", 8), ("norm_g", 8), ("mem_g", 8), ("dw_b", 8), ("ln_g", 8),
            ("ln_b", 8), ("dqn", 1), ("dkn", 1), ("subln", 1), ("xqn", 2), ("xkn", 2)]
VEC = {}
_at = 0
for _name, _count in VEC_ROWS:
    VEC[_name] = (_at, _count)
    _at += _count
NVEC = 96

CHUNKS = [("mk", j) for j in range(8)] + [("mv", j) for j in range(8)]
CHUNKS += [("fa", 0), ("qa", 0)] + [("va", j) for j in range(4)] + [("ka", 0)]
FOX_FILL = []
for _c in range(3):
    FOX_FILL += [("qa", _c + 1), ("ka", _c + 1), ("za", _c), ("zb", _c)]
FOX_FILL += [("kb", 0), ("vb", 0), ("za", 3), ("zb", 3)]
CHUNKS += FOX_FILL + [("qb", 0), ("qb", 1), ("qb", 2), ("qb", 3)]
CHUNKS += [("wo", j) for j in range(8)] + [("dq", 0), ("dk", 0)] + [("dv", j) for j in range(8)]
for _j in range(8):
    if _j < 7:
        CHUNKS += [("dq", _j + 1), ("dk", _j + 1)]
    CHUNKS += [("gb", _j), ("ga", _j), ("dg", _j)]


def _branch(b, between=()):
    out = [("m" + b, 0), ("m" + b, 1)] + list(between)
    for j in range(8):
        out.append(("p" + b, j))
        if j + 2 < 8:
            out.append(("m" + b, j + 2))
    return out


CHUNKS += _branch("d", [("xq", 0), ("xq", 1)])
for _h in range(4):
    if _h < 3:
        CHUNKS += [("xq", 2 * _h + 2), ("xq", 2 * _h + 3)]
    CHUNKS += [("xg", 2 * _h), ("xg", 2 * _h + 1)]
CHUNKS += _branch("x") + [("cg", j) for j in range(8)] + _branch("c") + [("w2", j) for j in range(8)]
SIGNALS = {
    "const_in": "loads of constants", "rows_in": "packed rows loaded by ScalarE's queue",
    "more_rows_in": "packed rows loaded by GpSimd's queue", "rows_clear": "the packed rows' memory is zeroed",
    "mem_in": "memory loaded", "x_in": "x loaded", "bcast_in": "vectors loaded on every partition",
    "rot_in": "rotation's permutation loaded", "x_again": "x loaded for the residual",
    "kvm_out": "memory's keys and values stored", "kvm_in": "and loaded again",
    "x1_out": "block 1's result stored", "x1_in": "and loaded again", "out_sem": "output stored",
    "w_hi": "weight chunks whose hi is there", "w_lo": "and whose lo is", "ada_used": "chunks of w_ada multiplied",
    "vec_done": "packed vectors scaled", "const_done": "constants converted", "eps_done": "eps there, then logarithms",
    "c_tanh": "tanh(c / 2)", "c_ready": "silu(c) on all columns", "lam_done": "lambda's sums, then exponentials",
    "mod_done": "shift and scale", "dve_step": "VectorE's own steps", "sumsq": "rows of squares summed",
    "ms_done": "mean squares of block 1's tail", "sqrt_done": "their roots", "rms_done": "1 / rms taken on ScalarE",
    "nk_done": "memory tiles normalised", "xn_done": "token tiles normalised (x, then x1)",
    "kvm_ready": "chunks of the memory's keys normalised", "h_hi": "chunks of a block's input: hi", "h_lo": "lo",
    "cum_dve": "forget gates' logits, then their cumulated logarithms", "cum_act": "ScalarE's steps between",
    "cum_hi": "hi of the negated cumulated logarithms", "cum_done": "lo", "rope_in": "reduced angles",
    "rope_out": "sine, cosine", "roped": "rotated keys and queries", "q_hi": "queries and keys: hi", "q_lo": "lo",
    "v_hi": "values: hi", "v_lo": "lo", "memk_hi": "memory's keys of a head: hi", "memk_lo": "lo",
    "negmax": "negated row maxima", "expd": "exponentials of sinks", "prob_ready": "units' probabilities",
    "pt_hi": "units' transposed probabilities: hi", "tanhed": "tanh of gates' arguments", "mixed": "gated outputs in mx",
    "o_hi": "gated output chunks: hi", "o_lo": "lo", "squared": "squares for sums over partitions",
    "qn_done": "queries and keys normalised", "of_copied": "squares of a differential head's output",
    "x1_done": "tiles of block 1's result", "conv_done": "chunks convolved", "ln_centred": "chunks less their mean",
    "ln_act": "their squares", "lnx": "their squares summed", "ln_scaled": "chunks over their deviation",
    "ln_t": "steps of ScalarE on them", "y_sum": "branch outputs added to y", "yhi": "chunks of y: hi", "ylo": "lo",
}
NCH = {name: n for n, name in enumerate(CHUNKS)}
PAIRED = ("mv", "va", "wo", "dv", "w2")
RAWS, SPLITS = 4, 4
NADA = 24
ADA_ENDS = [("ada", 4 * q + 3) for q in range(6)]
RAW = CHUNKS[:4]
for _i in range(6):
    RAW = RAW + CHUNKS[4 + 2 * _i:6 + 2 * _i] + [("ada", 4 * _i + j) for j in range(4)]
RAW = RAW + CHUNKS[16:]
NRAW = {name: n for n, name in enumerate(RAW)}


def plan_slots():
    slot, before, last, at = {}, {}, {}, 0
    for name in CHUNKS:
        if name[0] in PAIRED and name[1] % 2 == 0 and at % 2:
            at += 1
        slot[name] = at % SPLITS
        before[name] = last.get(at % SPLITS)
        last[at % SPLITS] = name
        at += 1
    return slot, before


SLOT, BEFORE = plan_slots()


def constants():
    k = np.zeros((P, K_COLS), np.float32)
    i = np.arange(P)
    k[:, K_IDENT:K_IDENT + P] = np.eye(P)
    k[:, K_BLOCKS:K_BLOCKS + P] = (i[:, None] // HD) == (i[None, :] // HD)
    k[:, K_ONES:K_ONES + P] = 1.0
    for o in range(P):
        if o % HD < HD // 2:
            k[o + HD // 2, K_ROT + o] = -1.0
        else:
            k[o - HD // 2, K_ROT + o] = 1.0
    k[:, K_CAUSAL:K_CAUSAL + P] = np.where(i[None, :] <= i[:, None], 0.0, MASKED)
    k[:, K_PREV:K_PREV + P] = np.where(i[None, :] > i[:, None], 0.0, MASKED)
    j = np.arange(S)
    k[:, K_DIST:K_DIST + S] = (j[None, :] - (S - P)) - i[:, None]
    k[:, K_FREQ] = (10000.0 ** (-(i % (HD // 2)).astype(np.float64) / (HD // 2))).astype(np.float32)
    return k


class Banks:

    def __init__(self, filled, emptied):
        self.filled, self.emptied = filled, emptied
        self.uses = [0] * len(filled)
        self.where = {}

    def open(self, pe, bank, key):
        self.uses[bank] += 1
        self.where[key] = (bank, self.uses[bank])
        if self.uses[bank] > 1:
            pe.wait_ge(self.emptied[bank], self.uses[bank] - 1)

    def close(self, ins, key):
        ins.then_inc(self.filled[self.where[key][0]], 1)

    def wait_full(self, eng, key):
        bank, n = self.where[key]
        eng.wait_ge(self.filled[bank], n)

    def empty(self, ins, key):
        ins.then_inc(self.emptied[self.where[key][0]], 1)

    def wait_empty(self, eng, key):
        bank, n = self.where[key]
        eng.wait_ge(self.emptied[bank], n)


def build(nc, t, out):
    ctx = ExitStack()
    with ctx:
        def sb(name, shape, dt=F32):
            return ctx.enter_context(nc.sbuf_tensor(name, shape, dt))

        def shared(*groups):
            got = []
            for n, group in enumerate(groups):
                with ExitStack() as own:
                    for spec in group:
                        if n < len(groups) - 1:
                            got.append(own.enter_context(nc.sbuf_tensor(*spec)))
                        else:
                            got.append(sb(*spec))
            return got

        def sem(name):
            return ctx.enter_context(nc.semaphore(name))

        raw = sb("raw", [P, RAWS, C, P])
        wh = sb("wh", [P, SPLITS, C, P], F32R)
        wl = sb("wl", [P, SPLITS, C, P], F32R)
        hh = sb("hh", [P, C, S], F32R)
        hl = sb("hl", [P, C, S], F32R)
        oh = sb("oh", [P, C, S], F32R)
        memx, xn, ol = shared([("memx", [P, 2, D], F32)], [("xn", [P, T, D], F32)], [("ol", [P, C, S], F32R)])
        va, vb, kvm, ytok, dv, x1r = shared([("va", [P, T, S], F32), ("vb", [P, T, P], F32)],
                                            [("kvm", [P, 2, 2 * D], F32)], [("ytok", [P, T, D], F32)],
                                            [("dv", [P, T, D], F32)], [("x1r", [P, T, D], F32)])
        km = kvm[:, 0, :].rearrange("p (c n) -> p c n", n=MEM)
        vm = kvm[:, 1, :].rearrange("p (t n) -> p t n", n=D)
        c_wide, _, bgate, negcum, sel, gate, u = shared(
            [("c_wide", [P, C, P], F32), ("beside", [P, 2 * D], F32), ("bgate", [P, D], F32)],
            [("negcum", [P, 2, S], F32R), ("sel", [P, 8, P], F32R), ("gate", [P, D], F32)],
            [("u", [P, C, PAD + S], F32)])
        cos, sin, gzb, rot, x, y = shared([("cos", [P, S], F32), ("sin", [P, S], F32), ("gzb", [P, 4, S], F32),
                                           ("rot", [P, P], F32)], [("x", [P, T, D], F32)], [("y", [P, C, S], F32)])
        ident = sb("ident", [P, P])
        ones = sb("ones", [P, P])
        masks = sb("masks", [P, 2, P], BF16)
        ident_b = sb("ident_b", [P, P], BF16)
        dist, slopes, blocks, xk = shared([("dist", [P, S], F16), ("slopes", [P, 8, P], F16), ("blocks", [P, P], F32)],
                                          [("xk", [P, 2, 2, MEM], F32R)])
        vec = sb("vec", [P, NVEC])
        taps = sb("taps", [P, TAPS * C])
        sc = sb("sc", [P, 116])
        rsm, prob = shared([("rsm", [P, 2 * S], F32)], [("prob", [P, 3, S], F32)])
        kload, gp, pth = shared([("kload", [P, K_COLS - K_PREV], F32), ("gp", [P, D], F32)], [("pth", [P, T, S], F32R)])
        vrows, cumt, ptl = shared([("vrows", [P, 3, P], F32)], [("cumt", [P, 4, S], F32)], [("ptl", [P, T, S], F32R)])
        th = sb("th", [P, S])
        norms = sb("norms", [P, 3, S])
        sq, rs = norms[:, 0, :], norms[:, 2, :]
        qf = sb("qf", [P, 2, S])
        qk = sb("qk", [P, 4, S], F32R)
        qh, ql, kh, kl = (qk[:, n, :] for n in range(4))
        gj = sb("gj", [P, S])
        mx = sb("mx", [P, S])
        pos, lam4, ca = shared([("pos", [P, S], I32), ("lam4", [P, 4, HD], F32)], [("ca", [P, 2, S], F32)])
        vv = sb("vv", [P, 2, T, P], F32R)
        vh, vl = vv[:, 0], vv[:, 1]
        stat = sb("stat", [P, 3, 16])
        MEM_SS, X_SS, Y_SS, X1_SS = sc[:, 0:2], sc[:, 2:6], sc[:, 6:10], sc[:, 10:14]
        freq, nlam, lsum = sc[:, 14:15], sc[:, 15:16], sc[:, 16:18]
        tc_, cc_ = sc[:, 18:26], sc[:, 26:34]
        modc, scale_a = sc[:, 34:50], sc[:, 50:58]
        sinks, nsinks, fbias = sc[:, 58:66], sc[:, 66:74], sc[0:8, 74:75]
        esink = sc[:, 80:96]
        y_parts, warm = sc[:, 98:114], sc[:, 114:115]
        eps6, eps5 = sc[:, 96:97], sc[:, 97:98]
        ps = [ctx.enter_context(nc.psum_tensor(f"bank{n}", [P, S], F32)) for n in range(8)]

        mem_scratch = nc.dram_tensor("mem_scratch", [P, 2, 2 * D], F32).ap()
        x1_scratch = nc.dram_tensor("x1_scratch", [P, T, D], F32).ap()

        banks = Banks([sem(f"filled{n}") for n in range(8)], [sem(f"emptied{n}") for n in range(8)])
        raw_loaded = [sem(f"raw_loaded{n}") for n in range(RAWS)]
        s = type("Signals", (), {name: sem(name) for name in SIGNALS})

        def v(name, j=0):
            return vec[:, VEC[name][0] + j:VEC[name][0] + j + 1]

        block = ctx.enter_context(nc.Block())

        def rows(w):
            return w.rearrange("(c p) n -> p c n", p=P)

        w_in, w_in_2, w_mem = rows(t["w_in"][0]), rows(t["w_in_2"][0]), rows(t["w_mem_kv_2"][0])
        w_ada, w_out_2 = rows(t["w_ada"][0]), rows(t["w_out_2"][0])
        projs = {"pd": rows(t["w_diff_proj_2"][0]), "px": rows(t["w_x_proj_2"][0]), "pc": rows(t["w_conv_proj_2"][0])}
        first = {"qa": 0, "ka": 512, "va": 1024, "fa": 1536, "za": 1544, "kb": 2568, "vb": 2696}
        second = {"ga": 0, "gb": 1024, "cg": 2048, "dq": 3072, "dk": 4096, "dv": 5120, "dg": 6144, "xq": 7168,
                  "xg": 8192, "mc": 9216, "md": 10240, "mx": 11264}

        def pieces(name):
            kind, j = name
            whole = lambda dst: dst
            if kind in ("mk", "mv"):
                at = j * P + (D if kind == "mv" else 0)
                return [(whole, w_mem[:, :, at:at + P])]
            if kind == "ada":
                return [(whole, w_ada[:, :, j * P:j * P + P])]
            if kind in projs:
                return [(whole, projs[kind][:, :, j * P:j * P + P])]
            if kind == "w2":
                return [(whole, w_out_2[:, :, j * P:j * P + P])]
            if kind in ("qb", "zb"):
                at = (2056 if kind == "qb" else 2824) + j * HD
                return [(lambda dst, i=i: dst[:, :, i * HD:i * HD + HD],
                         w_in[:, :, at + 256 * i:at + 256 * i + HD]) for i in range(2)]
            if kind == "wo":
                cols = slice(j * P, j * P + P)
                wo = t["w_out"][0]
                halves = [(lambda dst, i=i: dst[i * HD:i * HD + HD, 4:8, :],
                           wo[512 + 256 * i:768 + 256 * i, cols].rearrange("(c p) n -> p c n", p=HD)) for i in range(2)]
                return [(lambda dst: dst[:, 0:4, :], rows(wo[0:512, :])[:, :, cols])] + halves
            if kind in first:
                return [(whole, w_in[:, :, first[kind] + j * P:first[kind] + j * P + P])]
            return [(whole, w_in_2[:, :, second[kind] + j * P:second[kind] + j * P + P])]

        raw_count = [0] * RAWS
        raw_at = {}
        for n, name in enumerate(RAW):
            raw_count[n % RAWS] += 16 * len(pieces(name))
            raw_at[name] = (n % RAWS, raw_count[n % RAWS])

        def wait_raw(eng, name):
            slot, count = raw_at[name]
            eng.wait_ge(raw_loaded[slot], count)

        ada_count = {}
        done_by = {}

        @block.tensor
        def _(pe):
            proj_bank = [0]

            def next_bank(n=2):
                proj_bank[0] += 1
                return proj_bank[0] % n

            def three(o, a, b, start, stop, **kw):
                pe.matmul(o, a[0], b[1], start=start, stop=False, **kw)
                pe.matmul(o, a[1], b[0], start=False, stop=False, **kw)
                return pe.matmul(o, a[0], b[0], start=False, stop=stop, **kw)

            def chunk(name, act, nb=2, bank=None, fill=None, split=None):
                pe.wait_ge(s.w_lo, NCH[name] + 1)
                b = next_bank(nb) if bank is None else bank
                if fill is None:
                    banks.open(pe, b, name)
                o = ps[b][:] if fill is None else fill
                w = SLOT[name]
                for c in range(C):
                    if split is not None:
                        pe.wait_ge(split, c + 1)
                    ins = three(o, (wh[:, w, c, :], wl[:, w, c, :]), (act[0][:, c], act[1][:, c]), c == 0, c == C - 1)
                if fill is None:
                    banks.close(ins, name)
                    done_by[name] = name
                return ins

            H = (hh, hl)
            O = (oh, ol)

            def by_token(kind, g, act, tiles, nb=2, split=None):
                name = (kind, 2 * g)
                pe.wait_ge(s.w_lo, NCH[(kind, 2 * g + 1)] + 1)
                w = SLOT[name]
                for pair in range(tiles // 2):
                    key = (kind, g, pair)
                    b = next_bank(nb)
                    banks.open(pe, b, key)
                    for tt in range(2):
                        tok = slice((2 * pair + tt) * P, (2 * pair + tt + 1) * P)
                        for c in range(C):
                            if split is not None and (pair, tt) == (0, 0):
                                pe.wait_ge(split, c + 1)
                            ins = three(ps[b][:, 256 * tt:256 * tt + 256], (act[0][:, c, tok], act[1][:, c, tok]),
                                        (wh[:, w:w + 2, c, :], wl[:, w:w + 2, c, :]), c == 0, c == C - 1)
                    banks.close(ins, key)
                done_by[name] = done_by[(kind, 2 * g + 1)] = key

            def total(key, squares, ones_, n=S, bank=7):
                banks.open(pe, bank, key)
                for i, x_ in enumerate(squares):
                    ins = pe.matmul(ps[bank][:, 0:n], ones_[:], x_, start=i == 0, stop=i == len(squares) - 1)
                banks.close(ins, key)

            pe.wait_ge(s.const_in, 16 * 4)
            pe.wait_ge(s.rows_in, 16 * 11)
            pe.wait_ge(s.more_rows_in, 16 * 5)
            banks.open(pe, 7, "vec")
            banks.close(pe.transpose(ps[7][:, 0:NVEC], vrows[0:NVEC, 0, :], ident[0:NVEC, 0:NVEC]), "vec")
            banks.open(pe, 6, "taps")
            for i in range(2):
                ins = pe.transpose(ps[6][:, 124 * i:124 * i + 124], vrows[0:124, 1 + i, :], ident[0:124, 0:124])
            banks.close(ins, "taps")

            pe.wait_ge(s.nk_done, 2)
            for g in range(4):
                banks.open(pe, 2 + g, ("memT", g))
                for cc in range(2):
                    for tt in range(2):
                        ins = pe.transpose(ps[2 + g][:, (2 * cc + tt) * P:(2 * cc + tt + 1) * P],
                                           memx[:, tt, (2 * g + cc) * P:(2 * g + cc + 1) * P], ident[:])
                banks.close(ins, ("memT", g))
            MT = (hh[:, :, 0:MEM], hl[:, :, 0:MEM])
            for g in range(4):
                banks.wait_empty(pe, ("memT", g))
            def pieces(names, at, n, act=H):
                for piece in range(at, min(at + n, C * len(names))):
                    name, c = names[piece // C], piece % C
                    if c == 0:
                        pe.wait_ge(s.w_lo, NCH[name] + 1)
                        banks.open(pe, next_bank(), name)
                        done_by[name] = name
                    b, w = banks.where[name][0], SLOT[name]
                    if name[0] == "vb":
                        tok = slice(c // 2 * P, c // 2 * P + P)
                        for cc in range(4 * (c % 2), 4 * (c % 2) + 4):
                            ins = three(ps[b][:, tok], (act[0][:, cc, tok], act[1][:, cc, tok]),
                                        (wh[:, w, cc, :], wl[:, w, cc, :]), cc == 0, cc == C - 1)
                    else:
                        ins = three(ps[b][:], (wh[:, w, c, :], wl[:, w, c, :]), (act[0][:, c], act[1][:, c]),
                                    c == 0, c == C - 1)
                    if c == C - 1:
                        banks.close(ins, name)

            def modulation(j):
                name, q = ("ada", j), j // 4
                wait_raw(pe, name)
                if j == 0:
                    pe.wait_ge(s.c_ready, 1)
                if j % 4 == 0:
                    banks.open(pe, 4 + q % 3, ADA_ENDS[q])
                rows_ = 1 if q < 4 else P
                o = ps[4 + q % 3][0:rows_, j % 4 * P:j % 4 * P + P]
                for c in range(C):
                    ins = pe.matmul(o, c_wide[:, c, 0:rows_], raw[:, NRAW[name] % RAWS, c, :], start=c == 0, stop=c == C - 1)
                if name in ADA_ENDS:
                    banks.close(ins, name)
                else:
                    ins.then_inc(s.ada_used, 1)
                    ada_count[name] = len(ada_count) + 1

            for h in range(4):
                if h >= 2:
                    for j in range(4 * h - 8, 4 * h - 4):
                        modulation(j)
                b = next_bank()
                banks.open(pe, b, ("mk", h, "k"))
                for i in range(2):
                    ins = chunk(("mk", 2 * h + i), MT, bank=b, fill=ps[b][:, 256 * i:256 * i + 256])
                    done_by[("mk", 2 * h + i)] = ("mk", h, "k")
                banks.close(ins, ("mk", h, "k"))
                if h > 0:
                    pe.wait_ge(s.squared, h)
                    total(("mks", h - 1), [sq[:, 0:256], sq[:, 256:512]], ones, 256)
            for g in range(4):
                for j in range(4 * g + 8, 4 * g + 12):
                    modulation(j)
                by_token("mv", g, MT, 2)
                if g == 0:
                    pe.wait_ge(s.squared, 4)
                    total(("mks", 3), [sq[:, 0:256], sq[:, 256:512]], ones, 256)

            for q in range(4):
                banks.wait_empty(pe, ADA_ENDS[q])
            banks.open(pe, 7, "mod")
            for j in range(16):
                ins = pe.matmul(ps[7][:, j:j + 1], cumt[0:1, j // 4, j % 4 * P:j % 4 * P + P], ident[0:1, 0:1],
                                start=True, stop=True)
            banks.close(ins, "mod")

            def to_features(src, who, nb):
                for c in range(C):
                    b = 2 + c % nb
                    banks.open(pe, b, (who, c))
                    for tt in range(T):
                        ins = pe.transpose(ps[b][:, tt * P:tt * P + P], src[:, tt, c * P:c * P + P], ident[:])
                    banks.close(ins, (who, c))

            pe.wait_ge(s.xn_done, 4)
            to_features(xn, "xT", 3)

            chunk(("fa", 0), H, split=s.h_lo)
            chunk(("qa", 0), H)
            for g in range(2):
                by_token("va", g, H, T)
            chunk(("ka", 0), H)

            def fox_scores(h, tt):
                u_ = 4 * h + tt
                w = P * (tt + 1)
                b = 2 + u_ % 4
                half = slice(HD * (h % 2), HD * (h % 2) + HD)
                q_ = slice(tt * P, tt * P + P)
                if tt == 0 and h % 2 == 0:
                    pe.wait_ge(s.q_lo, 2 * (h // 2) + 2)
                if u_ == 0:
                    pe.wait_ge(s.cum_done, 1)
                    pe.wait_ge(s.const_done, 1)
                banks.open(pe, b, ("S", u_))
                o = ps[b][:, 0:w]
                three(o, (qh[half, q_], ql[half, q_]), (kh[half, 0:w], kl[half, 0:w]), True, False)
                pick = sel[0:8, h, :]
                pe.matmul(o, pick, negcum[0:8, 1, 0:w], start=False, stop=False)
                pe.matmul(o, pick, negcum[0:8, 0, 0:w], start=False, stop=True)
                ins = pe.matmul(ps[b][:, w - P:w], ident_b[:], masks[:, 1, :], start=False, stop=True, skip_group_check=True)
                banks.close(ins, ("S", u_))

            def turn(u_, key, src_blocks):
                pe.wait_ge(s.prob_ready, u_ + 1)
                banks.open(pe, 6, key)
                for n, blk in enumerate(src_blocks):
                    ins = pe.transpose(ps[6][:, n * P:n * P + P], blk, ident[:])
                banks.close(ins, key)

            def values_causal(key, v_count, last_pt):
                banks.wait_empty(pe, last_pt)
                pe.wait_ge(s.v_lo, v_count)
                banks.open(pe, 7, key)
                for kb in range(T):
                    ins = three(ps[7][:, kb * P:S], (vh[:, kb, :], vl[:, kb, :]),
                                (pth[:, kb, kb * P:S], ptl[:, kb, kb * P:S]), kb == 0, True, skip_group_check=True)
                banks.close(ins, key)

            def rotate(key):
                banks.wait_empty(pe, key)
                pe.wait_ge(s.rot_in, 16)
                banks.open(pe, 7, ("rot",) + key)
                banks.close(pe.matmul(ps[7][:], rot[:], qf[:, 0, :], start=True, stop=True), ("rot",) + key)

            def fox_turn(u_):
                turn(u_, ("PT", u_), [prob[:, u_ % 2, i * P:i * P + P] for i in range(u_ % 4 + 1)])

            queries = [("qb", i) for i in range(4)]
            for u_ in range(32):
                pieces(FOX_FILL, 4 * u_, 4)
                fox_scores(u_ // 4, u_ % 4)
                if u_ >= 2:
                    fox_turn(u_ - 2)
                if u_ >= 6 and u_ % 4 == 2:
                    h = u_ // 4 - 1
                    values_causal(("PO", h), h // 2 + 1, ("PT", 4 * h + 3))
                if u_ == 28:
                    rotate(("kb", 0))
            pieces(queries, 0, 4)
            fox_turn(30)
            pieces(queries, 4, 4)
            fox_turn(31)
            pieces(queries, 8, 2)
            rotate(("qb", 0))
            pieces(queries, 10, 2)
            values_causal(("PO", 7), 4, ("PT", 31))

            def swa_scores(n, i, g, tt):
                u_ = 32 + n
                b = 2 + u_ % 4
                half = slice(HD * g, HD * g + HD)
                q_ = slice(tt * P, tt * P + P)
                lo = max(tt - 1, 0) * P
                w = P if tt == 0 else 2 * P
                if n % 8 == 0:
                    pe.wait_ge(s.q_lo, 8 + i + 2)
                banks.open(pe, b, ("S", u_))
                o = ps[b][:, 2 * P - w:2 * P]
                three(o, (qh[half, q_], ql[half, q_]), (kh[half, lo:lo + w], kl[half, lo:lo + w]), True, False)
                m = masks[:, 2 - w // P:2, :]
                ins = pe.matmul(o, ident_b[:], m, start=False, stop=True)
                banks.close(ins, ("S", u_))

            for n in range(32 + 3):
                i, k = divmod(n, 8)
                if n < 32:
                    if k < 4:
                        if i == 0:
                            pieces(queries, 12 + k, 1)
                        else:
                            pieces(queries, 8 + 8 * i + 2 * k, 2)
                    swa_scores(n, i, k // 4, k % 4)
                if k == 6 and i < 3:
                    rotate(("qb", i + 1))
                if 0 <= n - 2 < 32:
                    u_ = 32 + n - 2
                    src = [prob[:, u_ % 2, P * j:P * j + P] for j in (range(2) if u_ % 4 else [1])]
                    turn(u_, ("PT", u_), src)
                if n >= 6 and n % 4 == 2:
                    h = 8 + n // 4 - 1
                    banks.wait_empty(pe, ("PT", 4 * h + 3))
                    pe.wait_ge(s.v_lo, 5)
                    banks.open(pe, 7, ("PO", h))
                    for kb in range(T):
                        w = P if kb == T - 1 else 2 * P
                        ins = three(ps[7][:, kb * P:kb * P + w], (vh[:, kb, :], vl[:, kb, :]),
                                    (pth[:, kb, kb * P:kb * P + w], ptl[:, kb, kb * P:kb * P + w]),
                                    kb == 0, True, skip_group_check=True)
                    banks.close(ins, ("PO", h))

            pe.wait_ge(s.o_lo, 7)
            pe.wait_ge(s.w_lo, NCH[("wo", 1)] + 1)
            w = SLOT[("wo", 0)]
            held = [next_bank(4) for _ in range(T)]
            for tt in range(T):
                banks.open(pe, held[tt], ("wo", 0, tt))
            for late in (range(0, C - 1), [C - 1]):
                if late == [C - 1]:
                    pe.wait_ge(s.o_lo, 8)
                for tt in range(T):
                    tok = slice(tt * P, tt * P + P)
                    for c in late:
                        ins = three(ps[held[tt]][:, 0:256], (oh[:, c, tok], ol[:, c, tok]),
                                    (wh[:, w:w + 2, c, :], wl[:, w:w + 2, c, :]), c == 0, c == C - 1)
                    if late == [C - 1]:
                        banks.close(ins, ("wo", 0, tt))
            done_by[("wo", 0)] = done_by[("wo", 1)] = ("wo", 0, 3)
            for g in range(1, 4):
                by_token("wo", g, O, T, 4)

            pe.wait_ge(s.xn_done, 8)
            to_features(ytok, "x1T", 4)
            for c in range(4, 8):
                banks.wait_empty(pe, ("x1T", c))
            chunk(("dq", 0), H)
            chunk(("dk", 0), H)
            for g in range(4):
                by_token("dv", g, H, T)
                if g < 2:
                    pe.wait_ge(s.squared, 4 + 1 + g)
                    total(("dns", g), [norms[:, g, :]], blocks)

            def diff_scores(j, tt):
                u_ = 4 * j + tt
                w = P * (tt + 1)
                q_ = slice(tt * P, tt * P + P)
                if tt == 0:
                    pe.wait_ge(s.q_lo, 13 + 2 * j + 2)
                for m in range(2):
                    b = 2 + 2 * (u_ % 2) + m
                    half = slice(HD * m, HD * m + HD)
                    banks.open(pe, b, ("D", u_, m))
                    o = ps[b][:, 0:w]
                    three(o, (qh[half, q_], ql[half, q_]), (kh[half, 0:w], kl[half, 0:w]), True, False)
                    pe.matmul(o, slopes[:, j, :], dist[:, S - w:S], start=False, stop=True)
                    ins = pe.matmul(ps[b][:, w - P:w], ident_b[:], masks[:, 1, :], start=False, stop=True,
                                    skip_group_check=True)
                    banks.close(ins, ("D", u_, m))

            def diff_turn(u_):
                turn(64 + u_, ("DT", u_), [prob[:, u_ % 2, i * P:i * P + P] for i in range(u_ % 4 + 1)])

            def diff_values(j):
                values_causal(("DO", j), 6 + j, ("DT", 4 * j + 3))

            def subln(j):
                pe.wait_ge(s.of_copied, j + 1)
                total(("sub", j), [rs], ones)

            for j in range(8):
                fill = ([("dq", j + 1), ("dk", j + 1)] if j < 7 else []) + [("gb", j), ("ga", j), ("dg", j)]
                for tt in range(4):
                    at, half = (10 * tt, 5) if j < 7 else ((0, 8, 12, 16)[tt], (4, 2, 2, 4)[tt])
                    for i in range(2):
                        pieces(fill, at + min(2, half // 2) * i, min(2, half // 2))
                        if tt == 3 and j < 7:
                            pe.wait_ge(s.squared, 4 + 2 + 2 * j + i + 1)
                            total(("dns", 2 * j + 2 + i), [norms[:, i, :]], blocks)
                    if half == 5:
                        pieces(fill, at + 4, 1)
                    diff_scores(j, tt)
                    pieces(fill, at + half, 2)
                    if tt == 1 and j > 0:
                        diff_values(j - 1)
                    pieces(fill, at + half + 2, half - 2)
                    if tt == 1 and j > 0:
                        subln(j - 1)
                    if 4 * j + tt > 0:
                        diff_turn(4 * j + tt - 1)
            pieces([("md", 0)], 0, 5)
            diff_turn(31)
            pieces([("md", 0)], 5, 3)
            diff_values(7)

            def branch(b, o_count):
                pe.wait_ge(s.o_lo, o_count)
                for j in range(8):
                    if (b, j) == ("d", 2):
                        xq_sums(0)
                    chunk(("p" + b, j), O, 4)
                    if j + 2 < 8:
                        chunk(("m" + b, j + 2), H, 4)

            chunk(("md", 1), H, 4)
            subln(7)
            for i in range(2):
                chunk(("xq", i), H, 4)

            def xq_sums(h):
                pe.wait_ge(s.squared, 4 + 16 + h + 1)
                total(("xns", h), [norms[:, 0, :], norms[:, 1, :]], ones)

            branch("d", 16)

            def x_scores(h, pr):
                u_ = 2 * h + pr
                b = 2 + u_ % 4
                if pr == 0:
                    pe.wait_ge(s.q_lo, 29 + 2 * h + 2)
                    pe.wait_ge(s.memk_lo, h + 1)
                banks.open(pe, b, ("X", u_))
                for tt in range(2):
                    q_ = slice((2 * pr + tt) * P, (2 * pr + tt + 1) * P)
                    o = ps[b][:, 256 * tt:256 * tt + 256]
                    three(o, (qh[:, q_], ql[:, q_]), (xk[:, 0, 0, :], xk[:, 1, 0, :]), True, False)
                    ins = three(o, (kh[:, q_], kl[:, q_]), (xk[:, 0, 1, :], xk[:, 1, 1, :]), False, True)
                banks.close(ins, ("X", u_))

            def x_turn(u_):
                src = [prob[:, u_ % 2, 256 * tt + kb * P:256 * tt + kb * P + P] for kb in range(2) for tt in range(2)]
                turn(96 + u_, ("XT", u_), src)

            def x_values(h):
                banks.wait_empty(pe, ("XT", 2 * h + 1))
                pe.wait_ge(s.v_lo, 14 + h)
                for i in range(2):
                    banks.open(pe, 7, ("XO", h, i))
                    for kb in range(2):
                        ins = three(ps[7][:], (vh[:, 2 * kb + i, :], vl[:, 2 * kb + i, :]),
                                    (pth[:, kb, :], ptl[:, kb, :]), kb == 0, kb == 1)
                    banks.close(ins, ("XO", h, i))

            for h in range(4):
                for pr in range(2):
                    if h == 3 and pr == 0:
                        x_turn(5)
                        chunk(("xg", 6), H)
                        x_values(2)
                    elif pr == 0:
                        chunk(("xq", 2 * h + 2), H)
                    elif h < 3:
                        chunk(("xg", 2 * h), H)
                        if h > 0:
                            x_values(h - 1)
                    else:
                        chunk(("xg", 7), H)
                    x_scores(h, pr)
                    if pr == 0 and h < 3:
                        chunk(("xq", 2 * h + 3), H)
                    if pr == 1 and h < 3:
                        chunk(("xg", 2 * h + 1), H)
                        xq_sums(h + 1)
                    if 2 * h + pr not in (0, 6):
                        x_turn(2 * h + pr - 1)
            gates = [("mx", 0), ("mx", 1)]
            pieces(gates, 0, 8)
            x_turn(7)
            pieces(gates, 8, 3)
            x_values(3)
            pieces(gates, 11, 5)
            branch("x", 24)

            pe.wait_ge(s.conv_done, 8)
            total("ln_sum", [u[:, j, PAD:] for j in range(C)], ones)
            chunk(("cg", 0), H)
            banks.open(pe, 7, "ln_var")
            for j in range(C):
                pe.wait_ge(s.ln_act, j + 1)
                ins = pe.matmul(ps[7][:], ones[:], sq if j % 2 == 0 else mx[:], start=j == 0, stop=j == C - 1)
                if j < C - 1:
                    ins.then_inc(s.lnx, 1)
            banks.close(ins, "ln_var")
            for j in range(1, 8):
                chunk(("cg", j), H)
            for i in range(2):
                chunk(("mc", i), H, 4)
            branch("c", 32)

            for g in range(4):
                by_token("w2", g, H, T, 4, s.ylo if g == 0 else None)

        @block.sync
        def _(sp):
            for n, name in enumerate(RAW):
                if n >= RAWS:
                    last = RAW[n - RAWS]
                    if last[0] != "ada":
                        sp.wait_ge(s.w_lo, NCH[last] + 1)
                    elif last in ADA_ENDS:
                        banks.wait_full(sp, last)
                    else:
                        sp.wait_ge(s.ada_used, ada_count[last])
                if n == 2:
                    sp.dma_start(memx[:], t["mem_2"][0].rearrange("(t p) d -> p t d", p=P)).then_inc(s.mem_in, 16)
                slot = n % RAWS
                for where, src in pieces(name):
                    sp.dma_start(where(raw[:, slot]), src).then_inc(raw_loaded[slot], 16)

        vector_rows = []
        for name, src in (("mem_g", "mem_norm_g_2"), ("c", "c"), ("b_ada", "b_ada"), ("g_pre", "g_pre"),
                          ("norm_g", "norm_g_2"), ("dw_b", "conv_dw_b_2"), ("ln_g", "conv_ln_g_2"),
                          ("ln_b", "conv_ln_b_2"), ("subln", "diff_subln_g_2"), ("xqn", "x_qn_g_2"), ("xkn", "x_kn_g_2")):
            a, n = VEC[name]
            vector_rows.append((vrows[a:a + n, 0, :], t[src][:, 0:n * P].rearrange("a (r p) -> (a r) p", p=P)))
        for name, src in (("dqn", "diff_qn_g_2"), ("dkn", "diff_kn_g_2")):
            for i in range(2):
                vector_rows.append((vrows[VEC[name][0]:VEC[name][0] + 1, 0, HD * i:HD * i + HD], t[src]))
        vector_rows.append((vrows[0:124, 1:3, :], t["conv_dw_2"][0].rearrange("k (j p) -> (k j) p", p=P)
                            .rearrange("(a r) p -> r a p", a=2)))

        @block.gpsimd
        def _(pool):
            pool.dma_start(ident[:], t["consts"][:, K_IDENT:K_IDENT + P]).then_inc(s.const_in, 16)
            pool.dma_start(kload[:], t["consts"][:, K_PREV:K_COLS]).then_inc(s.const_in, 16)
            pool.dma_start(ones[:], t["consts"][:, K_ONES:K_ONES + P]).then_inc(s.const_in, 16)
            pool.dma_start(blocks[:], t["consts"][:, K_BLOCKS:K_BLOCKS + P]).then_inc(s.const_in, 16)
            pool.wait_ge(s.rows_clear, 1)
            for dst, src in vector_rows[11:]:
                pool.dma_start(dst, src).then_inc(s.more_rows_in, 16)
            pool.dma_start(x[:], t["x"][0].rearrange("(t p) d -> p t d", p=P)).then_inc(s.x_in, 16)
            pool.dma_start(gp[:], t["g_post"].partition_broadcast(P)).then_inc(s.bcast_in, 16)
            pool.dma_start(bgate[:], t["b_ada"][:, 2 * D:3 * D].partition_broadcast(P)).then_inc(s.bcast_in, 16)
            for n, name in enumerate(("lambda_q1_2", "lambda_k1_2", "lambda_q2_2", "lambda_k2_2")):
                pool.dma_start(lam4[:, n, :], t[name].partition_broadcast(P)).then_inc(s.bcast_in, 16)
            pool.dma_start(sinks[:], t["sinks"].partition_broadcast(P)).then_inc(s.bcast_in, 16)
            pool.dma_start(fbias[:], t["b_fgate"].rearrange("a h -> h a")).then_inc(s.bcast_in, 16)
            pool.dma_start(pos[:], t["positions"].partition_broadcast(P)).then_inc(s.bcast_in, 16)
            pool.wait_ge(s.xn_done, 4)
            pool.dma_start(rot[:], t["consts"][:, K_ROT:K_ROT + P]).then_inc(s.rot_in, 16)
            pool.wait_ge(s.kvm_ready, 8)
            banks.wait_empty(pool, ("mv", 3, 0))
            pool.dma_start(mem_scratch, kvm[:]).then_inc(s.kvm_out, 16)
            pool.wait_ge(s.o_lo, 8)
            pool.dma_start(x[:], t["x"][0].rearrange("(t p) d -> p t d", p=P)).then_inc(s.x_again, 16)
            pool.wait_ge(s.x1_done, 4)
            pool.dma_start(x1_scratch, x[:]).then_inc(s.x1_out, 16)
            pool.wait_ge(s.v_lo, 13)
            pool.wait_ge(s.kvm_out, 16)
            pool.dma_start(kvm[:], mem_scratch).then_inc(s.kvm_in, 16)
            pool.wait_ge(s.v_lo, 17)
            pool.wait_ge(s.memk_lo, 4)
            pool.wait_ge(s.x1_out, 16)
            pool.dma_start(x1r[:], x1_scratch).then_inc(s.x1_in, 16)
            o_view = out[0].rearrange("(t p) d -> p t d", p=P)
            for g in range(4):
                for pair in range(2):
                    banks.wait_empty(pool, ("w2", g, pair))
                    pool.dma_start(o_view[:, 2 * pair:2 * pair + 2, 256 * g:256 * g + 256],
                                   x1r[:, 2 * pair:2 * pair + 2, 256 * g:256 * g + 256]).then_inc(s.out_sem, 16)
            pool.wait_ge(s.out_sem, 16 * 8)

        def v8(name):
            return vec[:, VEC[name][0]:VEC[name][0] + VEC[name][1]]

        def pt_key(n):
            return ("PT", n) if n < 64 else ("DT", n - 64) if n < 96 else ("XT", n - 96)

        roots = {}

        def wo_banks(g):
            if g == 0:
                return [(("wo", 0, tt), [tt]) for tt in range(T)]
            return [(("wo", g, pair), [2 * pair, 2 * pair + 1]) for pair in range(2)]

        @block.scalar
        def _(act):
            split = [0]
            rms = [0]
            th_free = [None]
            eps_and_logs = [1]

            def ahead(name):
                while split[0] < len(CHUNKS):
                    nxt = CHUNKS[split[0]]
                    prev = BEFORE[nxt]
                    if prev is not None:
                        if name is None or NCH[prev] > NCH[name]:
                            return
                        banks.wait_full(act, done_by[prev])
                    wait_raw(act, nxt)
                    act.activation(wh[:, SLOT[nxt]], raw[:, NRAW[nxt] % RAWS], ACT.Copy).then_inc(s.w_hi, 1)
                    split[0] += 1

            def roots_of(*sums):
                for key, dst, n in sums:
                    banks.wait_full(act, key)
                    banks.empty(act.activation(dst, ps[7][:], ACT.Ln, scale=1.0 / n, bias=eps6), key)
                for key, dst, n in sums:
                    banks.wait_empty(act, key)
                    act.activation(dst, dst, ACT.Exp, scale=-0.5).then_inc(s.rms_done, 1)
                    rms[0] += 1
                    roots[key] = rms[0]

            def root(who, dst, src, n, eps, key=None):
                ins = act.activation(dst, src, ACT.Ln, scale=1.0 / n, bias=eps)
                if key is None:
                    ins.then_inc(s.eps_done, 1)
                    eps_and_logs[0] += 1
                    act.wait_ge(s.eps_done, eps_and_logs[0])
                else:
                    banks.empty(ins, key)
                    banks.wait_empty(act, key)
                act.activation(dst, dst, ACT.Exp, scale=-0.5).then_inc(s.rms_done, 1)
                rms[0] += 1
                roots[who] = rms[0]

            def root_of(key, dst, n, eps=eps6):
                banks.wait_full(act, key)
                root(key, dst, ps[7][:], n, eps, key)

            def tanh_of(key):
                if th_free[0] is not None:
                    banks.wait_empty(act, th_free[0])
                banks.wait_full(act, key)
                return act.activation(th[:], ps[banks.where[key][0]][:], ACT.Tanh, scale=0.5)

            def gate_of(key):
                tanh_of(key).then_inc(s.tanhed, 1)
                th_free[0] = key
                ahead(key)

            junk = qf[:].rearrange("p a n -> p (a n)")
            squares = [0]

            def square_rows(src, dst, tiles):
                for tt in range(tiles):
                    if squares[0]:
                        act.wait_ge(s.sumsq, squares[0])
                    act.activation(junk, src[:, tt, :], ACT.Square, accum_out=dst[:, tt:tt + 1]).then_inc(s.sumsq, 1)
                    squares[0] += 1

            act.wait_ge(s.rows_clear, 1)
            for dst, src in vector_rows[:11]:
                act.dma_start(dst, src).then_inc(s.rows_in, 16)
            ahead(None)
            act.wait_ge(s.mem_in, 16)
            square_rows(memx, MEM_SS, 2)
            banks.wait_full(act, "vec")
            ins = act.activation(vec[:], ps[7][:, 0:NVEC], ACT.Copy)
            banks.empty(ins, "vec")
            act.wait_ge(s.eps_done, 1)
            act.wait_ge(s.sumsq, 2)
            root("mem", MEM_SS, MEM_SS, D, eps6)
            act.wait_ge(s.vec_done, 1)
            act.activation(tc_, v8("c"), ACT.Tanh, scale=0.5).then_inc(s.c_tanh, 1)
            for g in range(4):
                banks.wait_full(act, ("memT", g))
                for i in range(2):
                    c = 2 * g + i
                    act.activation(hh[:, c, 0:MEM], ps[2 + g][:, MEM * i:MEM * i + MEM], ACT.Identity,
                                   scale=v("mem_g", c)).then_inc(s.h_hi, 1)
            act.wait_ge(s.x_in, 16)
            square_rows(x, X_SS, T)
            act.wait_ge(s.sumsq, 6)
            root("x", X_SS, X_SS, D, eps6)
            act.wait_ge(s.lam_done, 1)
            act.activation(lsum, lsum, ACT.Exp).then_inc(s.lam_done, 1)
            def mem_log(h):
                key = ("mks", h)
                banks.wait_full(act, key)
                banks.empty(act.activation(rsm[:, MEM * h:MEM * h + MEM], ps[7][:, 0:MEM], ACT.Ln, scale=1.0 / MEM,
                                           bias=eps6), key)

            def modulation_row(q):
                banks.wait_full(act, ADA_ENDS[q])
                banks.empty(act.activation(cumt[0:1, q, :], ps[4 + q % 3][0:1, :], ACT.Copy), ADA_ENDS[q])

            for h in range(4):
                if h >= 2:
                    modulation_row(h - 2)
                key = ("mk", h, "k")
                b = banks.where[key][0]
                banks.wait_full(act, key)
                if h > 0:
                    mem_log(h - 1)
                act.activation(sq, ps[b][:], ACT.Square).then_inc(s.squared, 1)
                banks.empty(act.activation(km[:, 2 * h:2 * h + 2, :], ps[b][:].rearrange("p (c n) -> p c n", n=MEM),
                                           ACT.Copy), key)
                ahead(("mk", 2 * h + 1))
            for g in range(4):
                if g < 2:
                    modulation_row(2 + g)
                key = ("mv", g, 0)
                if g == 1:
                    mem_log(3)
                b = banks.where[key][0]
                banks.wait_full(act, key)
                banks.empty(act.activation(vm[:, :, MEM * g:MEM * g + MEM], ps[b][:].rearrange("p (c n) -> p c n", n=MEM),
                                           ACT.Copy), key)
                ahead(("mv", 2 * g + 1))
            banks.wait_empty(act, ("mks", 3))
            act.activation(rsm[:], rsm[:], ACT.Exp, scale=-0.5).then_inc(s.rms_done, 1)
            rms[0] += 1
            roots["rsm"] = rms[0]
            act.wait_ge(s.mod_done, 1)
            for c in range(C):
                key = ("xT", c)
                tmp = (mx, gj)[c % 2]
                banks.wait_full(act, key)
                if c >= 2:
                    act.wait_ge(s.h_lo, c - 1)
                banks.empty(act.activation(tmp[:], ps[banks.where[key][0]][:], ACT.Identity, scale=scale_a[:, c:c + 1],
                                           bias=modc[:, c:c + 1]), key)
                banks.wait_empty(act, key)
                act.activation(hh[:, c, :], tmp[:], ACT.Copy).then_inc(s.h_hi, 1)
            act.wait_ge(s.cum_dve, 1)
            f, e, l, cum = (cumt[0:8, n, :] for n in range(4))
            act.activation(e, f, ACT.Abs).then_inc(s.cum_act, 1)
            act.wait_ge(s.cum_act, 1)
            act.activation(e, e, ACT.Exp, scale=-1.0).then_inc(s.cum_act, 1)
            act.wait_ge(s.cum_act, 2)
            act.activation(e, e, ACT.Ln, bias=ones[0:8, 0:1]).then_inc(s.cum_act, 1)
            ahead(("fa", 0))

            def raw_q(key, i, free, next_=True):
                banks.wait_full(act, key)
                act.wait_ge(s.q_lo, free)
                banks.empty(act.activation(qf[:, i, :], ps[banks.where[key][0]][:], ACT.Copy), key)
                if next_:
                    ahead(key)

            raw_q(("qa", 0), 0, 0)
            act.wait_ge(s.kvm_out, 16)
            for g in range(2):
                for pair in range(2):
                    key = ("va", g, pair)
                    banks.wait_full(act, key)
                    banks.empty(act.activation(va[:, 2 * pair:2 * pair + 2, 256 * g:256 * g + 256],
                                               ps[banks.where[key][0]][:].rearrange("p (t n) -> p t n", n=256),
                                               ACT.Copy), key)
                ahead(("va", 2 * g + 1))
            raw_q(("ka", 0), 1, 0)
            act.wait_ge(s.cum_dve, 2)
            act.activation(negcum[0:8, 0, :], cum, ACT.Copy, scale=-1.0).then_inc(s.cum_hi, 1)

            def split_q(i, src, last_scores, scale=1.0):
                if last_scores is not None:
                    banks.wait_full(act, last_scores)
                act.activation((qh, kh)[i], src, ACT.Copy, scale=scale).then_inc(s.q_hi, 1)

            def exp_unit(u_, key, w, sink=None):
                act.wait_ge(s.negmax, u_ + 1)
                if u_ >= 2:
                    banks.wait_full(act, pt_key(u_ - 2))
                b = banks.where[key][0]
                col = u_ % 16
                lo = 256 - w if sink is not None else 0
                banks.empty(act.activation(prob[:, u_ % 2, lo:lo + w], ps[b][:, lo:lo + w], ACT.Exp,
                                           bias=stat[:, 0, col:col + 1], accum_out=stat[:, 1, col:col + 1]), key)
                if sink is not None:
                    act.activation(esink[:, col:col + 1], sinks[:, sink:sink + 1], ACT.Exp,
                                   bias=stat[:, 0, col:col + 1]).then_inc(s.expd, 1)

            def pt_hi(u_, dst, last_values, view=None):
                key = pt_key(u_)
                banks.wait_full(act, key)
                if last_values is not None:
                    banks.wait_full(act, last_values)
                act.activation(dst, view, ACT.Copy).then_inc(s.pt_hi, 1)

            def split_v(src, last_values):
                if last_values is not None:
                    banks.wait_full(act, last_values)
                act.activation(vh, src, ACT.Copy).then_inc(s.v_hi, 1)

            def split_o(c, scale=0.5, last=None, mixed=None, parts=()):
                if last is not None:
                    banks.wait_full(act, last)
                if mixed is not None:
                    act.wait_ge(s.mixed, mixed)
                for key in parts:
                    banks.wait_empty(act, key)
                act.activation(oh[:, c, :], mx[:], ACT.Copy, scale=scale).then_inc(s.o_hi, 1)

            def fox_pt_hi(u_):
                n = u_ % 4
                pt_hi(u_, pth[:, 0:n + 1, n * P:n * P + P], ("PO", u_ // 4 - 1) if u_ >= 4 else None,
                      ps[6][:, 0:n * P + P].rearrange("p (b n) -> p b n", n=P))

            for i in range(2):
                banks.wait_empty(act, (("qa", "ka")[i], 0))
                split_q(i, qf[:, i, :], None, (0.125, 1.0)[i])
            for u_ in range(32):
                c, k = divmod(u_, 8)
                key = FOX_FILL[u_ // 2] if k % 2 else None
                if key and key[0] in ("za", "zb"):
                    tanh_of(key).then_inc(s.tanhed, 1)
                    th_free[0] = key
                if k == 7 and c < 3:
                    for i in range(2):
                        banks.wait_empty(act, (("qa", "ka")[i], c + 1))
                        split_q(i, qf[:, i, :], ("S", u_), (0.125, 1.0)[i])
                if k == 2 and c > 0:
                    split_v(va[:, :, c * P:c * P + P], ("PO", 2 * c - 1))
                if u_ == 3:
                    banks.wait_empty(act, ("va", 1, 1))
                    split_v(va[:, :, 0:P], None)
                exp_unit(u_, ("S", u_), P * (k % 4 + 1))
                if key and key[0] in ("qa", "ka", "kb"):
                    raw_q(key, 1 if key[0] == "ka" else 0, 2 * c + 2)
                elif key and key[0] == "vb":
                    banks.wait_full(act, key)
                    banks.empty(act.activation(vb[:].rearrange("p t n -> p (t n)"), ps[banks.where[key][0]][:], ACT.Copy),
                                key)
                    ahead(key)
                elif key:
                    ahead(key)
                if u_ >= 2:
                    fox_pt_hi(u_ - 2)
                if k == 3 and c > 0:
                    split_o(c - 1, parts=[("PO", 2 * c - 2), ("PO", 2 * c - 1)])
                if u_ in (13, 17):
                    n = (u_ - 13) // 4
                    act.wait_ge(s.rope_in, n + 1)
                    act.activation((sin, cos)[n][:], gzb[:, 2, :], ACT.Sin).then_inc(s.rope_out, 1)
            fox_pt_hi(30)
            fox_pt_hi(31)
            act.wait_ge(s.roped, 1)
            raw_q(("qb", 0), 0, 8)
            split_q(1, qf[:, 1, :], ("S", 31))
            banks.wait_empty(act, ("vb", 0))
            split_v(vb[:], ("PO", 7))
            split_o(3, parts=[("PO", 6), ("PO", 7)])
            act.wait_ge(s.roped, 2)
            split_q(0, qf[:, 1, :], None, 0.125)

            for n in range(32 + 3):
                i, k = divmod(n, 8)
                if n < 32:
                    if k == 7 and i < 3:
                        act.wait_ge(s.roped, i + 3)
                        split_q(0, qf[:, 1, :], ("S", 32 + n), 0.125)
                    exp_unit(32 + n, ("S", 32 + n), P if k % 4 == 0 else 2 * P, sink=i + 4 * (k // 4))
                    if k == 3 and i < 3:
                        banks.wait_full(act, ("rot", "qb", i))
                        raw_q(("qb", i + 1), 0, 10 + i, False)
                m = n - 2
                if 0 <= m < 32:
                    tt = m % 4
                    kb = max(tt - 1, 0)
                    pt_hi(32 + m, pth[:, kb:tt + 1, tt * P:tt * P + P], ("PO", 8 + m // 4 - 1),
                          ps[6][:, 0:(tt + 1 - kb) * P].rearrange("p (b n) -> p b n", n=P))
                if k == 3 and 0 < i < 4:
                    split_o(3 + i, parts=[("PO", 6 + 2 * i), ("PO", 7 + 2 * i)])
                if k == 4 and i < 3:
                    ahead(("qb", i + 1))
            split_o(7, parts=[("PO", 14), ("PO", 15)])

            act.activation(warm, eps6, ACT.Sqrt)
            act.wait_ge(s.q_lo, 13)
            for g in range(4):
                for key, tiles in wo_banks(g):
                    banks.wait_full(act, key)
                    for n, tt in enumerate(tiles):
                        if squares[0] > 6:
                            act.wait_ge(s.sumsq, squares[0])
                        act.activation(junk[:, 0:256], ps[banks.where[key][0]][:, 256 * n:256 * n + 256], ACT.Square,
                                       accum_out=y_parts[:, 4 * tt + g:4 * tt + g + 1]).then_inc(s.sumsq, 1)
                        squares[0] += 1
                ahead(("wo", 2 * g + 1))
            act.wait_ge(s.ms_done, 1)
            act.activation(Y_SS, Y_SS, ACT.Sqrt).then_inc(s.sqrt_done, 1)
            for tt in range(T):
                act.wait_ge(s.x1_done, tt + 1)
                square_rows(x[:, tt:tt + 1, :], X1_SS[:, tt:tt + 1], 1)
            act.wait_ge(s.ms_done, 2)
            act.activation(X1_SS, X1_SS, ACT.Sqrt).then_inc(s.sqrt_done, 1)
            for c in range(C):
                key = ("x1T", c)
                banks.wait_full(act, key)
                act.activation(hh[:, c, :], ps[banks.where[key][0]][:], ACT.Identity, scale=v("norm_g", c)).then_inc(s.h_hi, 1)
            def square_q(i):
                act.activation(norms[:, i, :], qf[:, i, :], ACT.Square).then_inc(s.squared, 1)

            for i, name in enumerate(("dq", "dk")):
                raw_q((name, 0), i, 13)
                banks.wait_empty(act, (name, 0))
                square_q(i)
            for g in range(4):
                for pair in range(2):
                    key = ("dv", g, pair)
                    banks.wait_full(act, key)
                    banks.empty(act.activation(dv[:, 2 * pair:2 * pair + 2, 256 * g:256 * g + 256],
                                               ps[banks.where[key][0]][:].rearrange("p (t n) -> p t n", n=256),
                                               ACT.Copy), key)
                ahead(("dv", 2 * g + 1))
                if g < 2:
                    roots_of((("dns", g), norms[:, g, :], HD))
                if g == 3:
                    act.wait_ge(s.qn_done, 2)
                    for i in range(2):
                        split_q(i, qf[:, i, :], ("S", 63))

            def of_copy(j):
                banks.wait_full(act, ("DO", j))
                act.wait_ge(s.o_lo, 8 + j)
                act.activation(rs, ps[7][:], ACT.Square).then_inc(s.of_copied, 1)
                banks.empty(act.activation(mx[:], ps[7][:], ACT.Copy), ("DO", j))

            def diff_pt_hi(u_):
                n = u_ % 4
                pt_hi(64 + u_, pth[:, 0:n + 1, n * P:n * P + P],
                      ("DO", u_ // 4 - 1) if u_ >= 4 else ("PO", 15),
                      ps[6][:, 0:n * P + P].rearrange("p (b n) -> p b n", n=P))

            for j in range(8):
                for tt in range(4):
                    u_ = 4 * j + tt
                    w = P * (tt + 1)
                    if tt == 0 and j > 0:
                        tanh_of(("dg", j - 1)).then_inc(s.tanhed, 1)
                        th_free[0] = ("dg", j - 1)
                    if tt == 3:
                        if j < 7:
                            act.wait_ge(s.qn_done, 2 * j + 4)
                            for i in range(2):
                                split_q(i, qf[:, i, :], ("D", u_, 1))
                    for m in range(2):
                        key = ("D", u_, m)
                        col = (2 * u_ + m) % 16
                        act.wait_ge(s.negmax, 64 + 2 * u_ + m + 1)
                        if m == 0:
                            banks.wait_full(act, pt_key(64 + u_ - 2))
                        elif u_ > 0:
                            act.wait_ge(s.prob_ready, 64 + u_)
                        banks.empty(act.activation(prob[:, u_ % 2 if m == 0 else 2, 0:w], ps[banks.where[key][0]][:, 0:w],
                                                   ACT.Exp, bias=stat[:, 0, col:col + 1],
                                                   accum_out=stat[:, 1, col:col + 1]), key)
                    if tt == 1 and j > 0:
                        of_copy(j - 1)
                    if tt == 0 and j > 0:
                        ahead(("dg", j - 1))
                    if tt < 2 and j < 7:
                        key = (("dq", "dk")[tt], j + 1)
                        raw_q(key, tt, 13 + 2 * j + 2)
                        banks.wait_empty(act, key)
                        square_q(tt)
                    if tt == 2:
                        banks.empty(tanh_of(("gb", j)), ("gb", j))
                        th_free[0] = ("ga", j)
                        act.activation(warm, eps6, ACT.Ln)
                    if u_ > 0:
                        diff_pt_hi(u_ - 1)
                    if tt == 2:
                        split_v(dv[:, :, j * P:j * P + P], ("DO", j - 1) if j else ("PO", 15))
                        roots_of(*([(("sub", j - 1), rs, P)] if j else []),
                                 *([(("dns", 2 * j + 2 + i), norms[:, i, :], HD) for i in range(2)] if j < 7 else []))
                        ahead(("gb", j))
                    if tt == 3:
                        if j > 0:
                            split_o(j - 1, last=("wo", 3, 1), mixed=j)
            gate_of(("dg", 7))
            diff_pt_hi(31)
            of_copy(7)

            def x_squares(h):
                for i in range(2):
                    banks.wait_empty(act, ("xq", 2 * h + i))
                act.activation(norms[:, 0, :], qf[:, 0, :], ACT.Square)
                act.activation(norms[:, 1, :], qf[:, 1, :], ACT.Square).then_inc(s.squared, 1)

            def x_split(h):
                act.wait_ge(s.qn_done, 16 + 2 * h + 2)
                last = ("X", 2 * h - 1) if h else ("D", 31, 1)
                for i in range(2):
                    split_q(i, qf[:, i, :], last)
                act.activation(xk[:, 0], km[:, 2 * h:2 * h + 2, :], ACT.Copy).then_inc(s.memk_hi, 1)

            def branch(b, tail=None):
                for j in range(8):
                    if (b, j) == ("d", 2):
                        root_of(("xns", 0), rs, 256)
                    if (b, j) == ("d", 4):
                        act.wait_ge(s.kvm_in, 16)
                        x_split(0)
                    banks.empty(tanh_of(("m" + b, j)), ("m" + b, j))
                    th_free[0] = ("p" + b, j)
                    ahead(("m" + b, j))
                    if j == 0 and tail:
                        tail()
                    banks.wait_full(act, ("p" + b, j))
                    ahead(("p" + b, j))

            def diff_tail():
                root_of(("sub", 7), rs, P)
                split_o(7, mixed=8)
                for i in range(2):
                    raw_q(("xq", i), i, 29)
                x_squares(0)

            branch("d", diff_tail)


            def x_pt_hi(u_):
                pr = u_ % 2
                pt_hi(96 + u_, pth[:, 0:2, 256 * pr:256 * pr + 256], ("XO", u_ // 2 - 1, 1) if u_ >= 2 else ("DO", 7),
                      ps[6][:].rearrange("p (b n) -> p b n", n=256))

            def x_split_o(h):
                for i in range(2):
                    split_o(2 * h + i, last=("pd", 7), parts=[("XO", h, i)])

            for h in range(4):
                if h > 0:
                    x_split(h)
                for pr in range(2):
                    u_ = 2 * h + pr
                    if pr == 0 and h < 3:
                        raw_q(("xq", 2 * h + 2), 0, 29 + 2 * h + 2)
                    if (h, pr) == (3, 0):
                        x_pt_hi(5)
                    if (h, pr) in ((0, 1), (1, 1), (2, 1), (3, 0)):
                        gate_of(("xg", 2 * h))
                        if h > 0:
                            x_split_o(h - 1)
                    key = ("X", u_)
                    act.wait_ge(s.negmax, 128 + u_ + 1)
                    banks.wait_full(act, pt_key(96 + u_ - 2))
                    for tt in range(2):
                        col = (2 * u_ + tt) % 16
                        ins = act.activation(prob[:, u_ % 2, 256 * tt:256 * tt + 256],
                                             ps[banks.where[key][0]][:, 256 * tt:256 * tt + 256], ACT.Exp,
                                             bias=stat[:, 0, col:col + 1], accum_out=stat[:, 1, col:col + 1])
                    banks.empty(ins, key)
                    if pr == 0 and h < 3:
                        raw_q(("xq", 2 * h + 3), 1, 29 + 2 * h + 2)
                        x_squares(h + 1)
                    if pr == 1:
                        split_v(vm[:, :, MEM * h:MEM * h + MEM].rearrange("p k (i n) -> p k i n", n=P),
                                ("XO", h - 1, 1) if h else ("DO", 7))
                        gate_of(("xg", 2 * h + 1))
                        if h < 3:
                            root_of(("xns", h + 1), rs, 256)
                    if u_ not in (0, 6):
                        x_pt_hi(u_ - 1)
            x_pt_hi(7)
            x_split_o(3)
            branch("x")

            for j in range(C):
                act.wait_ge(s.ln_centred, j + 1)
                if j >= 2:
                    act.wait_ge(s.lnx, j - 1)
                elif j == 0:
                    act.wait_ge(s.o_lo, 24)
                act.activation((sq, mx[:])[j % 2], u[:, j, PAD:], ACT.Square).then_inc(s.ln_act, 1)
            root_of("ln_var", rs, D, eps5)
            for j in range(C):
                gate_of(("cg", j))
                act.wait_ge(s.ln_scaled, j + 1)
                if j > 0:
                    act.wait_ge(s.mixed, 8 + j)
                act.activation(qf[:, 0, :], u[:, j, PAD:], ACT.Identity, scale=v("ln_g", j), bias=v("ln_b", j))\
                   .then_inc(s.ln_t, 1)
                act.wait_ge(s.ln_t, 2 * j + 1)
                act.activation(qf[:, 1, :], qf[:, 0, :], ACT.Tanh, scale=0.5).then_inc(s.ln_t, 1)
                split_o(j, 0.25, ("px", 7), mixed=8 + j + 1)
            def y_hi(j):
                act.wait_ge(s.y_sum, 8 + j + 1)
                act.activation(hh[:, j, :], y[:, j, :], ACT.Copy, scale=0.5).then_inc(s.yhi, 1)

            for j in range(8):
                banks.empty(tanh_of(("mc", j)), ("mc", j))
                th_free[0] = ("pc", j)
                ahead(("mc", j))
                if j == 7:
                    for i in range(6):
                        y_hi(i)
                banks.wait_full(act, ("pc", j))
                ahead(("pc", j))
            y_hi(6)
            y_hi(7)
            for g in range(4):
                for pair in range(2):
                    banks.wait_full(act, ("w2", g, pair))
                ahead(("w2", 2 * g + 1))

        @block.vector
        def _(dve):
            split = [0]
            rms = [0]
            steps = [0]
            gates = [0]

            def then(ins):
                steps[0] += 1
                ins.then_inc(s.dve_step, 1)
                dve.wait_ge(s.dve_step, steps[0])

            def bank(key):
                return ps[banks.where[key][0]]

            def ahead(name):
                while split[0] < len(CHUNKS):
                    n = split[0]
                    nxt = CHUNKS[n]
                    prev = BEFORE[nxt]
                    if prev is not None and (name is None or NCH[prev] > NCH[name]):
                        return
                    dve.wait_ge(s.w_hi, n + 1)
                    w = SLOT[nxt]
                    dve.tensor_tensor(wl[:, w], raw[:, NRAW[nxt] % RAWS], wh[:, w].bitcast(F32), ALU.subtract)\
                       .then_inc(s.w_lo, 1)
                    split[0] += 1

            def wait_root(who):
                dve.wait_ge(s.rms_done, roots[who])

            dve.memset(vrows[:], 0.0).then_inc(s.rows_clear, 1)
            dve.memset(eps6, 1e-6)
            dve.memset(eps5, 1e-5).then_inc(s.eps_done, 1)
            ahead(None)
            dve.wait_ge(s.const_in, 16 * 4)
            dve.tensor_copy(masks[:].rearrange("p a n -> p (a n)"), kload[:, 0:2 * P])
            dve.tensor_copy(ident_b[:], ident[:])
            dve.tensor_copy(dist[:], kload[:, K_DIST - K_PREV:K_DIST - K_PREV + S])
            dve.tensor_copy(freq, kload[:, K_FREQ - K_PREV:K_FREQ - K_PREV + 1])
            for j in range(8):
                ins = dve.tensor_scalar(slopes[:, j, :], ident[:], 2.0 ** -(j + 1), None, ALU.mult)
            then(ins)
            wait_root("mem")
            for tt in range(2):
                dve.tensor_scalar(memx[:, tt, :], memx[:, tt, :], MEM_SS[:, tt:tt + 1], None, ALU.mult).then_inc(s.nk_done, 1)
            banks.wait_full(dve, "taps")
            banks.empty(dve.tensor_scalar(taps[:], ps[6][:, 0:TAPS * C], 0.5, None, ALU.mult), "taps")
            banks.wait_empty(dve, "vec")
            dve.tensor_scalar(v("dqn"), v("dqn"), HD ** -0.5, None, ALU.mult)
            dve.tensor_scalar(v8("xqn"), v8("xqn"), 256 ** -0.5, None, ALU.mult)
            dve.tensor_scalar(v("subln"), v("subln"), 1.0 - LAMBDA_INIT, None, ALU.mult).then_inc(s.vec_done, 1)
            dve.wait_ge(s.c_tanh, 1)
            then(dve.scalar_tensor_tensor(cc_, tc_, 1.0, v8("c"), ALU.add, ALU.mult))
            then(dve.tensor_scalar(cc_, cc_, 0.5, None, ALU.mult))
            for c in range(C):
                ins = dve.tensor_copy(c_wide[:, c, :], cc_[:, c:c + 1].to_broadcast([P, P]))
            ins.then_inc(s.c_ready, 1)
            for g in range(4):
                dve.wait_ge(s.h_hi, 2 * g + 2)
                for i in range(2):
                    c = 2 * g + i
                    ins = dve.scalar_tensor_tensor(hl[:, c, 0:MEM], ps[2 + g][:, MEM * i:MEM * i + MEM],
                                                   v("mem_g", c), hh[:, c, 0:MEM].bitcast(F32), ALU.mult, ALU.subtract)
                banks.empty(ins, ("memT", g))
            dve.wait_ge(s.bcast_in, 16 * 9)
            for i in range(2):
                ins = dve.tensor_tensor_reduce(gj[:, HD * i:HD * i + HD], lam4[:, 2 * i, :], lam4[:, 2 * i + 1, :], 1.0, 0.0,
                                               ALU.mult, ALU.add, lsum[:, i:i + 1])
            ins.then_inc(s.lam_done, 1)
            dve.wait_ge(s.lam_done, 2)
            then(dve.tensor_tensor(nlam, lsum[:, 1:2], lsum[:, 0:1], ALU.subtract))
            dve.tensor_scalar(nlam, nlam, -LAMBDA_INIT, None, ALU.add)
            dve.tensor_scalar(nsinks, sinks, -1.0, None, ALU.mult).then_inc(s.const_done, 1)
            dve.wait_ge(s.const_done, 1)
            wait_root("x")
            for tt in range(T):
                dve.tensor_scalar(xn[:, tt, :], x[:, tt, :], X_SS[:, tt:tt + 1], None, ALU.mult).then_inc(s.xn_done, 1)

            for h in range(4):
                banks.wait_full(dve, ("mk", h, "k"))
                ahead(("mk", 2 * h + 1))
            for g in range(4):
                banks.wait_full(dve, ("mv", g, 0))
                ahead(("mv", 2 * g + 1))
            banks.wait_full(dve, "mod")
            banks.empty(dve.tensor_tensor(modc, ps[7][:, 0:16], v8("b_ada"), ALU.add), "mod")
            banks.wait_empty(dve, "mod")
            dve.scalar_tensor_tensor(scale_a, modc[:, 8:16], 1.0, v8("g_pre"), ALU.add, ALU.mult).then_inc(s.mod_done, 1)
            for c in range(C):
                dve.wait_ge(s.h_hi, 8 + c + 1)
                dve.tensor_tensor(hl[:, c, :], (mx, gj)[c % 2][:], hh[:, c, :].bitcast(F32), ALU.subtract)\
                   .then_inc(s.h_lo, 1)
            wait_root("rsm")
            for c in range(C):
                banks.wait_empty(dve, ("mk", c // 2, "k"))
                dve.scalar_tensor_tensor(km[:, c, :], km[:, c, :], v("xkn", c % 2),
                                         rsm[:, MEM * (c // 2):MEM * (c // 2) + MEM], ALU.mult, ALU.mult)\
                   .then_inc(s.kvm_ready, 1)
            for k in range(2):
                banks.wait_full(dve, ADA_ENDS[4 + k])
            for k in range(2):
                cols = slice(S * k, S * k + S)
                banks.empty(dve.tensor_tensor(gate[:, cols], ps[5 + k][:], bgate[:, cols], ALU.add), ADA_ENDS[4 + k])
            for k in range(2):
                banks.wait_empty(dve, ADA_ENDS[4 + k])
            then(dve.tensor_tensor(gate[:], gate[:], gp[:], ALU.mult))
            for h in range(8):
                dve.tensor_copy(sel[0:8, h, :], ident[0:8, h:h + 1].to_broadcast([8, P]))
            f, e, l, cum = (cumt[0:8, n, :] for n in range(4))
            key = ("fa", 0)
            banks.wait_full(dve, key)
            banks.empty(dve.tensor_scalar(f, bank(key)[0:8, :], fbias, None, ALU.add), key)
            banks.wait_empty(dve, key)
            dve.memset(l, 1.0).then_inc(s.cum_dve, 1)
            ahead(key)
            dve.wait_ge(s.cum_act, 3)
            then(dve.scalar_tensor_tensor(e, f, 0.0, e, ALU.min, ALU.subtract))
            dve.tensor_tensor_scan(cum, l, e, 0.0, ALU.mult, ALU.add).then_inc(s.cum_dve, 1)
            banks.wait_full(dve, ("qa", 0))
            ahead(("qa", 0))
            for g in range(2):
                banks.wait_full(dve, ("va", g, 1))
                ahead(("va", 2 * g + 1))
            dve.wait_ge(s.cum_hi, 1)
            dve.scalar_tensor_tensor(negcum[0:8, 1, :], cum, -1.0, negcum[0:8, 0, :].bitcast(F32), ALU.mult, ALU.subtract)\
               .then_inc(s.cum_done, 1)
            banks.wait_full(dve, ("ka", 0))
            ahead(("ka", 0))

            def split_q(i, n, src, scale=1.0):
                dve.wait_ge(s.q_hi, n)
                dve.scalar_tensor_tensor((ql, kl)[i], src, scale, (qh, kh)[i].bitcast(F32), ALU.mult, ALU.subtract)\
                   .then_inc(s.q_lo, 1)

            def split_v(n, src):
                dve.wait_ge(s.v_hi, n)
                dve.tensor_tensor(vl, src, vh.bitcast(F32), ALU.subtract).then_inc(s.v_lo, 1)

            def split_o(c, n, scale=0.5):
                dve.wait_ge(s.o_hi, n)
                dve.scalar_tensor_tensor(ol[:, c, :], mx[:], scale, oh[:, c, :].bitcast(F32), ALU.mult, ALU.subtract)\
                   .then_inc(s.o_lo, 1)

            def gate_to(key, dst, free=True):
                gates[0] += 1
                dve.wait_ge(s.tanhed, gates[0])
                banks.wait_full(dve, key)
                banks.empty(dve.scalar_tensor_tensor(dst, th[:], 1.0, bank(key)[:], ALU.add, ALU.mult), key)
                if free:
                    banks.wait_empty(dve, key)
                    ahead(key)

            def normalise(u_, key, w, sink=False):
                col = u_ % 16
                lo = 256 - w if sink else 0
                r = stat[:, 2, col:col + 1]
                banks.wait_empty(dve, key)
                if sink:
                    dve.wait_ge(s.expd, u_ - 31)
                    then(dve.tensor_tensor(stat[:, 1, col:col + 1], stat[:, 1, col:col + 1], esink[:, col:col + 1], ALU.add))
                then(dve.reciprocal(r, stat[:, 1, col:col + 1]))
                dve.tensor_scalar(prob[:, u_ % 2, lo:lo + w], prob[:, u_ % 2, lo:lo + w], r, None, ALU.mult)\
                   .then_inc(s.prob_ready, 1)

            def pt_lo(u_, dst, hi, view):
                dve.wait_ge(s.pt_hi, u_ + 1)
                banks.empty(dve.tensor_tensor(dst, view, hi.bitcast(F32), ALU.subtract), pt_key(u_))

            def fox_pt_lo(u_):
                n = u_ % 4
                pt_lo(u_, ptl[:, 0:n + 1, n * P:n * P + P], pth[:, 0:n + 1, n * P:n * P + P],
                      ps[6][:, 0:n * P + P].rearrange("p (b n) -> p b n", n=P))

            def fox_mix(h):
                key = ("PO", h)
                half = slice(HD * (h % 2), HD * (h % 2) + HD)
                banks.wait_full(dve, key)
                if h >= 2:
                    dve.wait_ge(s.o_lo, h // 2)
                banks.empty(dve.tensor_tensor(mx[half, :], ps[7][half, :], gj[half, :], ALU.mult), key)

            def rope(key, splits):
                banks.wait_empty(dve, key)
                dve.wait_ge(s.q_lo, splits)
                dve.wait_ge(s.rope_out, 2)
                then(dve.tensor_tensor(qf[:, 1, :], qf[:, 0, :], cos[:], ALU.mult))
                banks.wait_full(dve, ("rot",) + key)
                banks.empty(dve.tensor_tensor(rs, ps[7][:], sin[:], ALU.mult), ("rot",) + key)
                banks.wait_empty(dve, ("rot",) + key)
                dve.tensor_tensor(qf[:, 1, :], qf[:, 1, :], rs, ALU.add).then_inc(s.roped, 1)

            def rotary_step(n):
                ang, turns, r = ca[:, 1, :], gzb[:, 3, :], gzb[:, 2, :]
                if n < 2:
                    then(dve.tensor_copy(ang, pos[:]) if n == 0 else dve.tensor_scalar(ang, ang, freq, None, ALU.mult))
                    return
                which, n = divmod(n - 2, 8)
                quarter = 0.25 * which
                if n == 0:
                    then(dve.tensor_scalar(turns, ang, 0.15915494309189535, quarter, ALU.mult, ALU.add))
                elif n < 3:
                    then(dve.tensor_scalar(turns, turns, (MAGIC, -MAGIC)[n - 1], None, ALU.add))
                elif n < 6:
                    if (which, n) == (1, 3):
                        dve.wait_ge(s.rope_out, 1)
                    part = (TWO_PI_A, TWO_PI_B, TWO_PI_C)[n - 3]
                    then(dve.scalar_tensor_tensor(r, turns, -part, ang if n == 3 else r, ALU.mult, ALU.add))
                elif n == 6:
                    then(dve.tensor_scalar(r, r, quarter * 2 * np.pi, PI, ALU.add, ALU.min))
                else:
                    dve.tensor_scalar(r, r, -PI, None, ALU.max).then_inc(s.rope_in, 1)

            for i in range(2):
                split_q(i, i + 1, qf[:, i, :], (0.125, 1.0)[i])
            for u_ in range(32):
                c, k = divmod(u_, 8)
                w = P * (k % 4 + 1)
                key = FOX_FILL[u_ // 2] if k % 2 else None
                if u_ > 0:
                    normalise(u_ - 1, ("S", u_ - 1), P * ((u_ - 1) % 4 + 1))
                if k == 7:
                    gate_to(key, gzb[:, c, :], False)
                if k == 5:
                    gate_to(key, gj[:], False)
                banks.wait_full(dve, ("S", u_))
                dve.reduce_max(stat[:, 0, u_ % 16:u_ % 16 + 1], bank(("S", u_))[:, 0:w], AX, negate=True)\
                   .then_inc(s.negmax, 1)
                if k == 7 and c < 3:
                    for i in range(2):
                        split_q(i, 2 * c + i + 3, qf[:, i, :], (0.125, 1.0)[i])
                if k == 2 and c > 0:
                    split_v(c + 1, va[:, :, c * P:c * P + P])
                if u_ == 3:
                    split_v(1, va[:, :, 0:P])
                if u_ >= 2:
                    fox_pt_lo(u_ - 2)
                if u_ >= 6 and u_ % 4 == 2:
                    fox_mix(u_ // 4 - 1)
                if k == 3 and c > 0:
                    for i in range(2):
                        banks.wait_empty(dve, ("PO", 2 * c - 2 + i))
                    split_o(c - 1, c)
                if key:
                    banks.wait_full(dve, key)
                    ahead(key)
                if u_ == 28:
                    rope(("kb", 0), 8)
                if 8 <= u_ < 17:
                    rotary_step(2 * u_ - 16)
                    rotary_step(2 * u_ - 15)
            normalise(31, ("S", 31), S)
            fox_pt_lo(30)
            banks.wait_full(dve, ("qb", 0))
            fox_pt_lo(31)
            split_q(1, 9, qf[:, 1, :])
            rope(("qb", 0), 9)
            split_v(5, vb[:])
            fox_mix(7)
            for i in range(2):
                banks.wait_empty(dve, ("PO", 6 + i))
            split_o(3, 4)
            split_q(0, 10, qf[:, 1, :], 0.125)
            ahead(("qb", 0))

            for n in range(32 + 3):
                i, k = divmod(n, 8)
                u_ = 32 + n
                if n < 32:
                    w = P if k % 4 == 0 else 2 * P
                    head = i + 4 * (k // 4)
                    m = stat[:, 0, u_ % 16:u_ % 16 + 1]
                    banks.wait_full(dve, ("S", u_))
                    then(dve.reduce_max(m, bank(("S", u_))[:, 256 - w:256], AX, negate=True))
                    dve.tensor_tensor(m, m, nsinks[:, head:head + 1], ALU.min).then_inc(s.negmax, 1)
                if 1 <= n < 33:
                    normalise(u_ - 1, ("S", u_ - 1), P if (n - 1) % 4 == 0 else 2 * P, True)
                if n < 32:
                    if k == 6 and i < 3:
                        rope(("qb", i + 1), 10 + i)
                    if k == 7 and i < 3:
                        split_q(0, 11 + i, qf[:, 1, :], 0.125)
                if 0 <= n - 2 < 32:
                    tt = (n - 2) % 4
                    kb = max(tt - 1, 0)
                    pt_lo(u_ - 2, ptl[:, kb:tt + 1, tt * P:tt * P + P], pth[:, kb:tt + 1, tt * P:tt * P + P],
                          ps[6][:, 0:(tt + 1 - kb) * P].rearrange("p (b n) -> p b n", n=P))
                if n >= 6 and n % 4 == 2:
                    h = n // 4 - 1
                    g = h % 2
                    key = ("PO", 8 + h)
                    half = slice(HD * g, HD * g + HD)
                    banks.wait_full(dve, key)
                    dve.wait_ge(s.o_lo, 4 + h // 2)
                    banks.empty(dve.tensor_tensor(mx[half, :], ps[7][half, :], gzb[half, h // 2, :], ALU.mult), key)
                if k == 4 and 0 < i < 4:
                    for g in range(2):
                        banks.wait_empty(dve, ("PO", 6 + 2 * i + g))
                    split_o(3 + i, 4 + i)
                if k == 5 and i < 3:
                    banks.wait_full(dve, ("qb", i + 1))
                    ahead(("qb", i + 1))
            for g in range(2):
                banks.wait_empty(dve, ("PO", 14 + g))
            split_o(7, 8)

            def small_root(n, sums, d):
                then(dve.tensor_scalar(sums, sums, 1.0 / d, None, ALU.mult))
                dve.tensor_scalar(sums, sums, 1e-6, None, ALU.add).then_inc(s.ms_done, 1)
                dve.wait_ge(s.sqrt_done, n)
                then(dve.reciprocal(sums, sums))

            squared = 6
            dve.wait_ge(s.v_lo, 5)
            for g in range(4):
                cols = slice(256 * g, 256 * g + 256)
                for key, tiles in wo_banks(g):
                    squared += len(tiles)
                    dve.wait_ge(s.sumsq, squared)
                    for n, tt in enumerate(tiles):
                        ins = dve.tensor_tensor(ytok[:, tt, cols], bank(key)[:, 256 * n:256 * n + 256], gate[:, cols], ALU.mult)
                    banks.empty(ins, key)
                ahead(("wo", 2 * g + 1))
            then(dve.reduce_sum(Y_SS, y_parts.rearrange("p (t g) -> p t g", g=4), AX))
            small_root(1, Y_SS, D)
            dve.wait_ge(s.x_again, 16)
            for pair in range(2):
                banks.wait_empty(dve, ("wo", 3, pair))
            for tt in range(T):
                dve.scalar_tensor_tensor(x[:, tt, :], ytok[:, tt, :], Y_SS[:, tt:tt + 1], x[:, tt, :], ALU.mult, ALU.add)\
                   .then_inc(s.x1_done, 1)
            dve.wait_ge(s.sumsq, squared + 4)
            small_root(2, X1_SS, D)
            for tt in range(T):
                dve.wait_ge(s.x1_done, tt + 1)
                dve.tensor_scalar(ytok[:, tt, :], x[:, tt, :], X1_SS[:, tt:tt + 1], None, ALU.mult).then_inc(s.xn_done, 1)
            for c in range(C):
                key = ("x1T", c)
                dve.wait_ge(s.h_hi, 16 + c + 1)
                banks.empty(dve.scalar_tensor_tensor(hl[:, c, :], bank(key)[:], v("norm_g", c),
                                                     hh[:, c, :].bitcast(F32), ALU.mult, ALU.subtract), key)
            for j in range(C):
                ins = dve.memset(u[:, j, 0:PAD], 0.0)
            then(ins)
            def norm_q(i, gain, key, r=None):
                wait_root(key)
                dve.scalar_tensor_tensor(qf[:, i, :], qf[:, i, :], gain, norms[:, i if r is None else r, :], ALU.mult,
                                         ALU.mult).then_inc(s.qn_done, 1)

            for i, name in enumerate(("dq", "dk")):
                banks.wait_full(dve, (name, 0))
                ahead((name, 0))
            for g in range(4):
                banks.wait_full(dve, ("dv", g, 1))
                ahead(("dv", 2 * g + 1))
                if g == 2:
                    norm_q(0, v("dqn"), ("dns", 0))
                    norm_q(1, v("dkn"), ("dns", 1))
                if g == 3:
                    for i in range(2):
                        split_q(i, 14 + i, qf[:, i, :])

            taps_done = [0]
            conv_count = [0, 0]

            def conv(n, glus):
                for _ in range(n):
                    j, k = divmod(taps_done[0], TAPS)
                    if j >= glus:
                        return
                    src, w, dst = u[:, j, k:k + S], taps[:, k * C + j:k * C + j + 1], ca[:, k % 2, :]
                    if k < 2:
                        if j > 0:
                            dve.wait_ge(s.conv_done, j)
                        ins = dve.tensor_scalar(dst, src, w, v("dw_b", j) if k == 0 else None, ALU.mult,
                                                *([ALU.add] if k == 0 else []))
                    else:
                        dve.wait_ge(s.dve_step, conv_count[k % 2])
                        ins = dve.scalar_tensor_tensor(dst, src, w, dst, ALU.mult, ALU.add)
                    steps[0] += 1
                    conv_count[k % 2] = steps[0]
                    ins.then_inc(s.dve_step, 1)
                    taps_done[0] += 1
                    if k == TAPS - 1:
                        dve.wait_ge(s.dve_step, steps[0])
                        dve.tensor_tensor(u[:, j, PAD:], ca[:, 0, :], ca[:, 1, :], ALU.add).then_inc(s.conv_done, 1)

            def diff_pt_lo(u_):
                n = u_ % 4
                pt_lo(64 + u_, ptl[:, 0:n + 1, n * P:n * P + P], pth[:, 0:n + 1, n * P:n * P + P],
                      ps[6][:, 0:n * P + P].rearrange("p (b n) -> p b n", n=P))

            def diff_mix(j):
                wait_root(("sub", j))
                banks.wait_empty(dve, ("DO", j))
                then(dve.scalar_tensor_tensor(mx[:], mx[:], v("subln"), rs, ALU.mult, ALU.mult))
                dve.tensor_tensor(mx[:], mx[:], gj[:], ALU.mult).then_inc(s.mixed, 1)
                return j

            for j in range(8):
                for tt in range(4):
                    u_ = 4 * j + tt
                    w = P * (tt + 1)
                    if tt == 0 and j > 0:
                        gate_to(("dg", j - 1), gj[:], False)
                    if tt == 3:
                        key = ("ga", j)
                        banks.wait_empty(dve, ("gb", j))
                        banks.wait_full(dve, key)
                        banks.empty(dve.scalar_tensor_tensor(u[:, j, PAD:], th[:], 1.0, bank(key)[:], ALU.add, ALU.mult), key)
                    for m in range(2):
                        col = (2 * u_ + m) % 16
                        banks.wait_full(dve, ("D", u_, m))
                        dve.reduce_max(stat[:, 0, col:col + 1], bank(("D", u_, m))[:, 0:w], AX, negate=True)\
                           .then_inc(s.negmax, 1)
                    if tt == 3 and j < 7:
                        for i in range(2):
                            split_q(i, 13 + 2 * (j + 1) + i + 1, qf[:, i, :])
                    if tt == 3 and j > 0:
                        diff_mix(j - 1)
                    if tt < 3:
                        conv(4, j)
                    col = 2 * u_ % 16
                    r = stat[:, 2, col:col + 2]
                    for m in range(2):
                        banks.wait_empty(dve, ("D", u_, m))
                    then(dve.reciprocal(r, stat[:, 1, col:col + 2]))
                    then(dve.tensor_tensor(r[:, 1:2], r[:, 1:2], nlam, ALU.mult))
                    p0 = prob[:, u_ % 2, 0:w]
                    then(dve.tensor_scalar(p0, p0, r[:, 0:1], None, ALU.mult))
                    dve.scalar_tensor_tensor(p0, prob[:, 2, 0:w], r[:, 1:2], p0, ALU.mult, ALU.add)\
                       .then_inc(s.prob_ready, 1)
                    if tt == 0 and j > 0:
                        banks.wait_full(dve, ("dg", j - 1))
                        ahead(("dg", j - 1))
                    if tt < 2 and j < 7:
                        key = (("dq", "dk")[tt], j + 1)
                        banks.wait_full(dve, key)
                        ahead(key)
                    if u_ > 0:
                        diff_pt_lo(u_ - 1)
                    if tt == 2:
                        split_v(6 + j, dv[:, :, j * P:j * P + P])
                        conv(4, j)
                    if tt == 2 and j < 7:
                        norm_q(0, v("dqn"), ("dns", 2 * j + 2))
                        norm_q(1, v("dkn"), ("dns", 2 * j + 3))
                    if tt == 2:
                        banks.wait_full(dve, ("gb", j))
                        ahead(("gb", j))
                    if tt == 3:
                        if j > 0:
                            dve.wait_ge(s.mixed, j)
                            split_o(j - 1, 8 + j)
            gate_to(("dg", 7), gj[:])
            diff_pt_lo(31)

            def branch(b, tail=None, filler=lambda: None):
                for j in range(8):
                    banks.wait_full(dve, ("m" + b, j))
                    ahead(("m" + b, j))
                    if j == 0 and tail:
                        tail()
                    if (b, j) == ("d", 2):
                        x_norm(0)
                    if (b, j) == ("d", 4):
                        x_split(0)
                    key = ("p" + b, j)
                    if (b, j) == ("c", 7):
                        for i in range(6):
                            y_lo(i)
                    banks.wait_empty(dve, ("m" + b, j))
                    banks.wait_full(dve, key)
                    dst = y[:, j, :] if b == "d" else gj[:]
                    added = {"d": 0, "x": j, "c": 8 + j}[b]
                    if added:
                        dve.wait_ge(s.y_sum, added)
                    banks.empty(dve.scalar_tensor_tensor(dst, th[:], 1.0, bank(key)[:], ALU.add, ALU.mult), key)
                    banks.wait_empty(dve, key)
                    ahead(key)
                    if b != "d":
                        dve.tensor_tensor(y[:, j, :], y[:, j, :], gj[:], ALU.add).then_inc(s.y_sum, 1)
                    filler()

            def diff_tail():
                diff_mix(7)
                dve.wait_ge(s.mixed, 8)
                split_o(7, 16)
                for i in range(2):
                    banks.wait_full(dve, ("xq", i))
                    ahead(("xq", i))
                dve.wait_ge(s.x1_out, 16)

            def x_split(h):
                for i in range(2):
                    split_q(i, 29 + 2 * h + i + 1, qf[:, i, :])
                dve.wait_ge(s.memk_hi, h + 1)
                dve.tensor_tensor(xk[:, 1], km[:, 2 * h:2 * h + 2, :], xk[:, 0].bitcast(F32), ALU.subtract)\
                   .then_inc(s.memk_lo, 1)

            def x_norm(h):
                norm_q(0, v("xqn", 0), ("xns", h), 2)
                norm_q(1, v("xqn", 1), ("xns", h), 2)

            branch("d", diff_tail, lambda: conv(9, 8))

            def x_mix(h):
                for i in range(2):
                    key = ("XO", h, i)
                    banks.wait_full(dve, key)
                    dve.wait_ge(s.o_lo, 16 + 2 * h + i)
                    banks.empty(dve.tensor_tensor(mx[:], ps[7][:], (gj[:], prob[:, 2, :])[i], ALU.mult), key)
                    banks.wait_empty(dve, key)
                    split_o(2 * h + i, 16 + 2 * h + i + 1)

            def x_pt_lo(u_):
                pr = u_ % 2
                cols = slice(256 * pr, 256 * pr + 256)
                pt_lo(96 + u_, ptl[:, 0:2, cols], pth[:, 0:2, cols], ps[6][:].rearrange("p (b n) -> p b n", n=256))

            for h in range(4):
                if h > 0:
                    x_split(h)
                for pr in range(2):
                    u_ = 2 * h + pr
                    if (h, pr) == (3, 0):
                        x_pt_lo(5)
                    if (h, pr) in ((0, 1), (1, 1), (2, 1), (3, 0)):
                        if h > 0:
                            x_mix(h - 1)
                        gate_to(("xg", 2 * h), gj[:])
                    if pr == 0 and h < 3:
                        banks.wait_full(dve, ("xq", 2 * h + 2))
                        ahead(("xq", 2 * h + 2))
                    key = ("X", u_)
                    col = 2 * u_ % 16
                    banks.wait_full(dve, key)
                    dve.reduce_max(stat[:, 0, col:col + 2], bank(key)[:].rearrange("p (t n) -> p t n", n=256), AX,
                                   negate=True).then_inc(s.negmax, 1)
                    if h > 0:
                        conv(5, 8)
                    banks.wait_empty(dve, key)
                    then(dve.reciprocal(stat[:, 2, col:col + 2], stat[:, 1, col:col + 2]))
                    for tt in range(2):
                        p = prob[:, u_ % 2, 256 * tt:256 * tt + 256]
                        ins = dve.tensor_scalar(p, p, stat[:, 2, col + tt:col + tt + 1], None, ALU.mult)
                    ins.then_inc(s.prob_ready, 1)
                    if pr == 0 and h < 3:
                        banks.wait_full(dve, ("xq", 2 * h + 3))
                        ahead(("xq", 2 * h + 3))
                    if pr == 1:
                        split_v(14 + h, vm[:, :, MEM * h:MEM * h + MEM].rearrange("p k (i n) -> p k i n", n=P))
                        gate_to(("xg", 2 * h + 1), prob[:, 2, :])
                        if h < 3:
                            x_norm(h + 1)
                    if u_ not in (0, 6):
                        x_pt_lo(u_ - 1)
            x_pt_lo(7)
            x_mix(3)
            branch("x", None, lambda: conv(7, 8))

            banks.wait_full(dve, "ln_sum")
            banks.empty(dve.tensor_scalar(rs, ps[7][:], 1.0 / D, None, ALU.mult), "ln_sum")
            banks.wait_empty(dve, "ln_sum")
            for j in range(C):
                dve.tensor_tensor(u[:, j, PAD:], u[:, j, PAD:], rs, ALU.subtract).then_inc(s.ln_centred, 1)
            banks.wait_full(dve, "ln_var")
            wait_root("ln_var")
            for j in range(C):
                dve.wait_ge(s.ln_centred, j + 1)
                dve.tensor_tensor(u[:, j, PAD:], u[:, j, PAD:], rs, ALU.mult).then_inc(s.ln_scaled, 1)
            for j in range(C):
                gate_to(("cg", j), gj[:])
                dve.wait_ge(s.ln_t, 2 * j + 2)
                then(dve.scalar_tensor_tensor(qf[:, 1, :], qf[:, 1, :], 1.0, qf[:, 0, :], ALU.add, ALU.mult))
                if j > 0:
                    dve.wait_ge(s.o_lo, 24 + j)
                dve.tensor_tensor(mx[:], qf[:, 1, :], gj[:], ALU.mult).then_inc(s.mixed, 1)
                dve.wait_ge(s.mixed, 8 + j + 1)
                split_o(j, 24 + j + 1, 0.25)

            def y_lo(j):
                dve.wait_ge(s.yhi, j + 1)
                dve.scalar_tensor_tensor(hl[:, j, :], y[:, j, :], 0.5, hh[:, j, :].bitcast(F32), ALU.mult, ALU.subtract)\
                   .then_inc(s.ylo, 1)

            branch("c")
            for j in (6, 7):
                y_lo(j)
            dve.wait_ge(s.x1_in, 16)
            for g in range(4):
                for pair in range(2):
                    key = ("w2", g, pair)
                    o = x1r[:, 2 * pair:2 * pair + 2, 256 * g:256 * g + 256]
                    banks.wait_full(dve, key)
                    banks.empty(dve.tensor_tensor(o, bank(key)[:].rearrange("p (t n) -> p t n", n=256), o, ALU.add), key)
                ahead(("w2", 2 * g + 1))


INPUTS = ["x", "c", "positions", "w_ada", "b_ada", "g_pre", "w_in", "b_fgate", "sinks", "w_out", "g_post", "mem_2",
          "norm_g_2", "mem_norm_g_2", "w_in_2", "conv_dw_2", "conv_dw_b_2", "conv_ln_g_2", "conv_ln_b_2",
          "w_conv_proj_2", "diff_qn_g_2", "diff_kn_g_2", "lambda_q1_2", "lambda_k1_2", "lambda_q2_2", "lambda_k2_2",
          "diff_subln_g_2", "w_diff_proj_2", "w_mem_kv_2", "x_qn_g_2", "x_kn_g_2", "w_x_proj_2", "w_out_2"]


def kernel(**inputs):
    import concourse.bacc as bacc
    from concourse.bass_utils import run_bass_kernel_spmd

    nc = bacc.Bacc("TRN2", target_bir_lowering=False, num_devices=1, dynamic_dma_scratch_size=1024)
    arrays, t = {}, {}
    for name in INPUTS:
        a = np.ascontiguousarray(inputs[name])
        arrays["in_" + name] = a
        t[name] = nc.dram_tensor("in_" + name, a.shape, mybir.dt.from_np(a.dtype), kind="ExternalInput").ap()
    arrays["in_consts"] = constants()
    t["consts"] = nc.dram_tensor("in_consts", (P, K_COLS), F32, kind="ExternalInput").ap()
    out = nc.dram_tensor("out_x", (1, S, D), F32, kind="ExternalOutput").ap()
    build(nc, t, out)
    r = run_bass_kernel_spmd(nc, [arrays], core_ids=[0])
    return r.results[0]["out_x"]
```
